# Optimizing a Trainium2 kernel written in Bass

```python
import jax, jax.numpy as jnp
from jax import lax
import numpy as np
import math

D_MODEL = 1024
BATCH = 1
SEQ = 256
DEPTH = 1

HEAD_DIM = 64
RWKV_HEADS = D_MODEL // HEAD_DIM
RWKV_WIDTH = RWKV_HEADS * HEAD_DIM
DECAY_LORA = 64
AAA_LORA = 64
GATE_LORA = 160
RWKV_COLS = 3 * RWKV_WIDTH + DECAY_LORA + AAA_LORA + GATE_LORA
GN_EPS = 64e-5
ATTN_PAIRS = ((128, 1), (512, 4), (2048, 16))
ATTN_GROUPS = 3
ATTN_HEADS_PER_GROUP = 4
ATTN_HEADS = ATTN_GROUPS * ATTN_HEADS_PER_GROUP
ATTN_WIDTH = ATTN_HEADS * HEAD_DIM
N_BRANCHES = 2
IN_COLS = RWKV_COLS + 3 * ATTN_WIDTH + N_BRANCHES * D_MODEL
D_FF = 2816
RMS_EPS = 1e-6
NEG_INF = -1e30


def _split_last(t, sizes):
    out, start = [], 0
    for n in sizes:
        out.append(t[..., start:start + n])
        start += n
    return out

def rms_norm(x, g):
    xf = x.astype(jnp.float32)
    y = xf * lax.rsqrt(jnp.mean(xf * xf, axis=-1, keepdims=True) + RMS_EPS)
    return y.astype(x.dtype) * g

def swiglu(h, w_in, w_out):
    gate, up = _split_last(h @ w_in, (D_FF, D_FF))
    return (jax.nn.silu(gate) * up) @ w_out

def token_shift(p, mu):
    prev = jnp.pad(p, ((0, 0), (1, 0), (0, 0)))[:, :-1]
    return p + (prev - p) * mu

def wkv7_scan(r, w, k, v, a, b):
    B, S, H, N = r.shape
    to_time = lambda t: jnp.moveaxis(t, 1, 0)

    def step(state, inp):
        r_t, w_t, k_t, v_t, a_t, b_t = inp
        sa = jnp.einsum('bhvk,bhk->bhv', state, a_t)
        state = (state * w_t[:, :, None, :] + sa[..., None] * b_t[:, :, None, :]
                 + v_t[..., None] * k_t[:, :, None, :])
        return state, jnp.einsum('bhvk,bhk->bhv', state, r_t)

    state0 = jnp.zeros((B, H, N, N), jnp.float32)
    _, out = lax.scan(step, state0, (to_time(r), to_time(w), to_time(k),
                                      to_time(v), to_time(a), to_time(b)))
    return jnp.moveaxis(out, 0, 1)

def rwkv7_time_mix(p, mu, w0, w2, a0, a2, g2, k_k, k_a, r_k, ln_w, ln_b):
    B, S, _ = p.shape
    H, N = RWKV_HEADS, HEAD_DIM
    p = token_shift(p.astype(jnp.float32), mu)
    r, k, v, wd, ad, gd = _split_last(
        p, (RWKV_WIDTH, RWKV_WIDTH, RWKV_WIDTH, DECAY_LORA, AAA_LORA, GATE_LORA))
    w = -jax.nn.softplus(-(w0 + jnp.tanh(wd) @ w2)) - 0.5
    decay = jnp.exp(-jnp.exp(w))
    a = jax.nn.sigmoid(a0 + ad @ a2)
    g = jax.nn.sigmoid(gd) @ g2
    heads = lambda t: t.reshape(B, S, H, N)
    kk = heads(k * k_k)
    kk = kk / jnp.maximum(jnp.sqrt(jnp.sum(kk * kk, axis=-1, keepdims=True)), 1e-12)
    k = k * (1.0 + (a - 1.0) * k_a)
    rh, kh, vh, ah = heads(r), heads(k), heads(v), heads(a)
    wkv = wkv7_scan(rh, heads(decay), kh, vh, -kk, kk * ah)
    mean = jnp.mean(wkv, axis=-1, keepdims=True)
    var = jnp.mean(jnp.square(wkv - mean), axis=-1, keepdims=True)
    y = ((wkv - mean) * lax.rsqrt(var + GN_EPS)).reshape(B, S, RWKV_WIDTH) * ln_w + ln_b
    bonus = jnp.sum(rh * kh * r_k, axis=-1, keepdims=True) * vh
    return (y + bonus.reshape(B, S, RWKV_WIDTH)) * g

def dilated_group_attention(q, k, v, window, dilation):
    B, S, Hg, E = q.shape
    span = window // dilation
    blk = span
    sub = S // dilation
    nb = -(-sub // blk)
    pad = nb * blk - sub

    def to_sub(t):
        t = t.reshape(B, sub, dilation, Hg, E).transpose(0, 2, 1, 3, 4)
        t = jnp.pad(t, ((0, 0), (0, 0), (0, pad), (0, 0), (0, 0)))
        return t.reshape(B, dilation, nb, blk, Hg, E)

    def with_prev(t):
        tp = jnp.pad(t, ((0, 0), (0, 0), (1, 0), (0, 0), (0, 0), (0, 0)))
        return jnp.concatenate([tp[:, :, :-1], tp[:, :, 1:]], axis=3)

    qb = to_sub(q)
    kw, vw = with_prev(to_sub(k)), with_prev(to_sub(v))
    s = jnp.einsum('bdnqhe,bdnkhe->bdnhqk', qb, kw)
    qi = jnp.arange(blk)[:, None]
    kj = jnp.arange(2 * blk)[None, :]
    dist = qi + blk - kj
    bidx = jnp.arange(nb)[:, None, None]
    valid = (dist >= 0) & (dist <= span) & (bidx * blk + kj - blk >= 0)
    s = jnp.where(valid[None, None, :, None], s, NEG_INF)
    m = jnp.max(s, axis=-1, keepdims=True)
    pexp = jnp.exp(s - m)
    den = jnp.sum(pexp, axis=-1, keepdims=True)
    o = jnp.einsum('bdnhqk,bdnkhe->bdnqhe', pexp / den, vw)
    lse = (m + jnp.log(den))[..., 0].transpose(0, 1, 2, 4, 3)
    o = o.reshape(B, dilation, nb * blk, Hg, E)[:, :, :sub]
    o = o.transpose(0, 2, 1, 3, 4).reshape(B, S, Hg, E)
    lse = lse.reshape(B, dilation, nb * blk, Hg)[:, :, :sub]
    lse = lse.transpose(0, 2, 1, 3).reshape(B, S, Hg)
    return o, lse

def dilated_attention(pq, pk, pv, q_gain, k_gain):
    B, S, _ = pq.shape
    heads = lambda t: t.astype(jnp.float32).reshape(B, S, ATTN_HEADS, HEAD_DIM)
    q = rms_norm(heads(pq), q_gain) * (HEAD_DIM ** -0.5)
    k = rms_norm(heads(pk), k_gain)
    v = heads(pv)
    outs, lses = [], []
    for gi, (window, dilation) in enumerate(ATTN_PAIRS):
        sl = slice(gi * ATTN_HEADS_PER_GROUP, (gi + 1) * ATTN_HEADS_PER_GROUP)
        o, lse = dilated_group_attention(q[:, :, sl], k[:, :, sl], v[:, :, sl], window, dilation)
        outs.append(o)
        lses.append(lse)
    o = jnp.stack(outs, axis=2)
    alpha = jax.nn.softmax(jnp.stack(lses, axis=2), axis=2)
    return (o * alpha[..., None]).reshape(B, S, ATTN_WIDTH)

def first_inputs(seed: int = 0) -> dict:
    key = jax.random.key(seed)
    ks = jax.random.split(key, 27)
    f32 = jnp.float32
    L, D = DEPTH, D_MODEL

    def nrm(k, shape, scale):
        return scale * jax.random.normal(k, shape, f32)

    def gain(k, shape):
        return 1.0 + 0.1 * jax.random.normal(k, shape, f32)

    return {
        'x': jax.random.normal(ks[0], (BATCH, SEQ, D), f32),
        'ffn1_norm': gain(ks[1], (L, D)),
        'ffn1_w_in': nrm(ks[2], (L, D, 2 * D_FF), D ** -0.5),
        'ffn1_w_out': nrm(ks[3], (L, D_FF, D), D_FF ** -0.5),
        'mix_norm': gain(ks[4], (L, D)),
        'w_in': nrm(ks[5], (L, D, IN_COLS), D ** -0.5),
        'b_gate': nrm(ks[6], (L, N_BRANCHES * D), 0.1),
        'rwkv_mu': jax.random.uniform(ks[7], (L, RWKV_COLS), f32),
        'rwkv_w0': jax.random.uniform(ks[8], (L, RWKV_WIDTH), f32, -6.0, 0.0),
        'rwkv_w2': nrm(ks[9], (L, DECAY_LORA, RWKV_WIDTH), 0.1 * DECAY_LORA ** -0.5),
        'rwkv_a0': nrm(ks[10], (L, RWKV_WIDTH), 0.1),
        'rwkv_a2': nrm(ks[11], (L, AAA_LORA, RWKV_WIDTH), AAA_LORA ** -0.5),
        'rwkv_g2': nrm(ks[12], (L, GATE_LORA, RWKV_WIDTH), GATE_LORA ** -0.5),
        'rwkv_k_k': gain(ks[13], (L, RWKV_WIDTH)),
        'rwkv_k_a': gain(ks[14], (L, RWKV_WIDTH)),
        'rwkv_r_k': nrm(ks[15], (L, RWKV_HEADS, HEAD_DIM), 0.1),
        'rwkv_ln_w': gain(ks[16], (L, RWKV_WIDTH)),
        'rwkv_ln_b': nrm(ks[17], (L, RWKV_WIDTH), 0.01),
        'attn_q_norm': gain(ks[18], (L, HEAD_DIM)),
        'attn_k_norm': gain(ks[19], (L, HEAD_DIM)),
        'w_proj_rwkv': nrm(ks[20], (L, RWKV_WIDTH, D), RWKV_WIDTH ** -0.5),
        'w_proj_attn': nrm(ks[21], (L, ATTN_WIDTH, D), ATTN_WIDTH ** -0.5),
        'w_out': nrm(ks[22], (L, D, D), D ** -0.5),
        'ffn2_norm': gain(ks[23], (L, D)),
        'ffn2_w_in': nrm(ks[24], (L, D, 2 * D_FF), D ** -0.5),
        'ffn2_w_out': nrm(ks[25], (L, D_FF, D), D_FF ** -0.5),
    }

def first_block(x, ffn1_norm, ffn1_w_in, ffn1_w_out, mix_norm, w_in, b_gate, rwkv_mu,
              rwkv_w0, rwkv_w2, rwkv_a0, rwkv_a2, rwkv_g2, rwkv_k_k, rwkv_k_a, rwkv_r_k,
              rwkv_ln_w, rwkv_ln_b, attn_q_norm, attn_k_norm, w_proj_rwkv, w_proj_attn,
              w_out, ffn2_norm, ffn2_w_in, ffn2_w_out):
    for l in range(DEPTH):
        x = x + 0.5 * swiglu(rms_norm(x, ffn1_norm[l]), ffn1_w_in[l], ffn1_w_out[l])
        h = rms_norm(x, mix_norm[l])
        p_rwkv, p_q, p_k, p_v, p_gate = _split_last(
            h @ w_in[l], (RWKV_COLS, ATTN_WIDTH, ATTN_WIDTH, ATTN_WIDTH, N_BRANCHES * D_MODEL))
        y_a = rwkv7_time_mix(p_rwkv, rwkv_mu[l], rwkv_w0[l], rwkv_w2[l], rwkv_a0[l],
                             rwkv_a2[l], rwkv_g2[l], rwkv_k_k[l], rwkv_k_a[l], rwkv_r_k[l],
                             rwkv_ln_w[l], rwkv_ln_b[l]).astype(x.dtype)
        y_b = dilated_attention(p_q, p_k, p_v, attn_q_norm[l], attn_k_norm[l]).astype(x.dtype)
        g_a, g_b = _split_last(jax.nn.sigmoid(p_gate + b_gate[l]), (D_MODEL, D_MODEL))
        merged = g_a * (y_a @ w_proj_rwkv[l]) + g_b * (y_b @ w_proj_attn[l])
        x = x + merged @ w_out[l]
        x = x + 0.5 * swiglu(rms_norm(x, ffn2_norm[l]), ffn2_w_in[l], ffn2_w_out[l])
    return x


DEPTH_2 = 2

PLE_DIM = 256
DIFF_HEADS = 8
DIFF_HEAD_DIM = 64
DIFF_V_DIM = 2 * DIFF_HEAD_DIM
MLA_HEADS = 8
MLA_Q_RANK = 384
MLA_KV_RANK = 256
MLA_NOPE_DIM = 64
MLA_ROPE_DIM = 32
MLA_V_DIM = 64
ROPE_THETA = 10000.0
REL_BUCKETS = 32
REL_MAX_DIST = 128
DENSE_FF = 2816
N_EXPERTS = 8
TOP_K = 2
EXPERT_FF = 3584
EXPERT_BLOCK = 128
Q_BLOCK = 128
EPS = 1e-5
DEEPNORM_ALPHA = (2.0 * DEPTH_2) ** 0.25
DEEPNORM_BETA = (8.0 * DEPTH_2) ** -0.25
N_DENSE = (DEPTH_2 + 1) // 2
N_MOE = DEPTH_2 // 2

DIFF_Q_COLS = DIFF_HEADS * 2 * DIFF_HEAD_DIM
DIFF_K_COLS = DIFF_HEADS * 2 * DIFF_HEAD_DIM
DIFF_V_COLS = DIFF_HEADS * DIFF_V_DIM
GATE_COLS = 2 * D_MODEL
IN_SIZES = (DIFF_Q_COLS, DIFF_K_COLS, DIFF_V_COLS, MLA_Q_RANK, MLA_KV_RANK, MLA_ROPE_DIM, GATE_COLS)
IN_SPLIT_IDX = [sum(IN_SIZES[:j + 1]) for j in range(len(IN_SIZES) - 1)]
IN_COLS_2 = sum(IN_SIZES)


def _layernorm(x, g, b):
    xf = x.astype(jnp.float32)
    mu = jnp.mean(xf, axis=-1, keepdims=True)
    var = jnp.mean(jnp.square(xf - mu), axis=-1, keepdims=True)
    y = (xf - mu) * lax.rsqrt(var + EPS) * g.astype(jnp.float32) + b.astype(jnp.float32)
    return y.astype(x.dtype)

def _rmsnorm(x, g):
    xf = x.astype(jnp.float32)
    y = xf * lax.rsqrt(jnp.mean(jnp.square(xf), axis=-1, keepdims=True) + EPS) * g.astype(jnp.float32)
    return y.astype(x.dtype)

def _rope(x, pos):
    half = x.shape[-1] // 2
    inv_freq = ROPE_THETA ** (-jnp.arange(half, dtype=jnp.float32) / half)
    ang = pos.astype(jnp.float32)[:, :, None] * inv_freq
    c = jnp.cos(ang)[:, :, None, :]
    s = jnp.sin(ang)[:, :, None, :]
    xf = x.astype(jnp.float32)
    x1, x2 = xf[..., :half], xf[..., half:]
    return jnp.concatenate([x1 * c - x2 * s, x1 * s + x2 * c], axis=-1).astype(x.dtype)

def _t5_bucket(dist):
    n = jnp.maximum(dist, 0)
    max_exact = REL_BUCKETS // 2
    large = max_exact + (jnp.log(jnp.maximum(n, 1).astype(jnp.float32) / max_exact)
                         / math.log(REL_MAX_DIST / max_exact) * (REL_BUCKETS - max_exact)).astype(jnp.int32)
    large = jnp.minimum(large, REL_BUCKETS - 1)
    return jnp.where(n < max_exact, n, large)

def _t5_bias(table, q_pos, k_pos):
    bucket = _t5_bucket(q_pos[:, :, None] - k_pos[:, None, :])
    return jnp.transpose(table[bucket].astype(jnp.float32), (0, 3, 1, 2))

def _causal_mask(q0, kend):
    return jnp.arange(kend)[None, :] <= (q0 + jnp.arange(Q_BLOCK))[:, None]

def _diff_attention(q, k, v, pos, rel_table, lam, lam_init, subln_g):
    B, S, H = q.shape[0], q.shape[1], q.shape[2]
    scale = DIFF_HEAD_DIM ** -0.5
    outs = []
    for q0 in range(0, S, Q_BLOCK):
        kend = q0 + Q_BLOCK
        s = jnp.einsum('bqhmd,bkhmd->bhmqk', q[:, q0:kend], k[:, :kend]).astype(jnp.float32) * scale
        s = s + _t5_bias(rel_table, pos[:, q0:kend], pos[:, :kend])[:, :, None]
        s = jnp.where(_causal_mask(q0, kend), s, -jnp.inf)
        a = jax.nn.softmax(s, axis=-1)
        w = a[:, :, 0] - lam * a[:, :, 1]
        outs.append(jnp.einsum('bhqk,bkhe->bqhe', w.astype(v.dtype), v[:, :kend]))
    o = jnp.concatenate(outs, axis=1)
    o = _rmsnorm(o, subln_g) * (1.0 - lam_init)
    return o.reshape(B, S, H * DIFF_V_DIM)

def _mla(c_q, c_kv, k_r, pos, q_norm_g, w_uq, kv_norm_g, w_ukv):
    B, S = c_q.shape[0], c_q.shape[1]
    q = (_rmsnorm(c_q, q_norm_g) @ w_uq).reshape(B, S, MLA_HEADS, MLA_NOPE_DIM + MLA_ROPE_DIM)
    q_nope, q_rope = q[..., :MLA_NOPE_DIM], _rope(q[..., MLA_NOPE_DIM:], pos)
    kv = (_rmsnorm(c_kv, kv_norm_g) @ w_ukv).reshape(B, S, MLA_HEADS, MLA_NOPE_DIM + MLA_V_DIM)
    k_nope, v = kv[..., :MLA_NOPE_DIM], kv[..., MLA_NOPE_DIM:]
    k_rope = _rope(k_r[:, :, None, :], pos)[:, :, 0]
    scale = (MLA_NOPE_DIM + MLA_ROPE_DIM) ** -0.5
    outs = []
    for q0 in range(0, S, Q_BLOCK):
        kend = q0 + Q_BLOCK
        s = (jnp.einsum('bqhd,bkhd->bhqk', q_nope[:, q0:kend], k_nope[:, :kend])
             + jnp.einsum('bqhr,bkr->bhqk', q_rope[:, q0:kend], k_rope[:, :kend])).astype(jnp.float32) * scale
        s = jnp.where(_causal_mask(q0, kend), s, -jnp.inf)
        a = jax.nn.softmax(s, axis=-1)
        outs.append(jnp.einsum('bhqk,bkhd->bqhd', a.astype(v.dtype), v[:, :kend]))
    return jnp.concatenate(outs, axis=1).reshape(B, S, MLA_HEADS * MLA_V_DIM)

def _mixer(h, pos, rel_table, w_in, b_gate, lq1, lk1, lq2, lk2, lam_init, diff_subln_g,
           mla_q_norm_g, w_uq, mla_kv_norm_g, w_ukv, w_branch_diff, w_branch_mla, w_out):
    B, S, _ = h.shape
    z = h @ w_in
    dq, dk, dv, cq, ckv, kr, gl = jnp.split(z, IN_SPLIT_IDX, axis=-1)
    lam = (jnp.exp(jnp.sum(lq1.astype(jnp.float32) * lk1.astype(jnp.float32)))
           - jnp.exp(jnp.sum(lq2.astype(jnp.float32) * lk2.astype(jnp.float32))) + lam_init)
    o_a = _diff_attention(dq.reshape(B, S, DIFF_HEADS, 2, DIFF_HEAD_DIM),
                          dk.reshape(B, S, DIFF_HEADS, 2, DIFF_HEAD_DIM),
                          dv.reshape(B, S, DIFF_HEADS, DIFF_V_DIM),
                          pos, rel_table, lam, lam_init, diff_subln_g)
    o_b = _mla(cq, ckv, kr, pos, mla_q_norm_g, w_uq, mla_kv_norm_g, w_ukv)
    g = jax.nn.sigmoid(gl + b_gate)
    g_a, g_b = g[..., :D_MODEL], g[..., D_MODEL:]
    m = g_a * (o_a @ w_branch_diff) + g_b * (o_b @ w_branch_mla)
    return m @ w_out

def _swiglu(x, w1, w3, w2):
    return (jax.nn.silu(x @ w1) * (x @ w3)) @ w2

def _moe(x, w_router, w1, w3, w2):
    B, S, D = x.shape
    xt = x.reshape(-1, D)
    T = xt.shape[0]
    M = T * TOP_K
    logits = (xt @ w_router).astype(jnp.float32)
    top_v, top_e = lax.top_k(logits, TOP_K)
    gates = jax.nn.softmax(top_v, axis=-1)
    flat_e = top_e.reshape(-1)
    flat_tok = jnp.repeat(jnp.arange(T, dtype=jnp.int32), TOP_K)
    order = jnp.argsort(flat_e, stable=True)
    se, stok, sg = flat_e[order], flat_tok[order], gates.reshape(-1)[order]
    counts = jnp.bincount(flat_e, length=N_EXPERTS)
    padded = ((counts + EXPERT_BLOCK - 1) // EXPERT_BLOCK) * EXPERT_BLOCK
    start = jnp.cumsum(counts) - counts
    pstart = jnp.cumsum(padded) - padded
    dest = pstart[se] + jnp.arange(M, dtype=jnp.int32) - start[se]
    n_blocks = -(-M // EXPERT_BLOCK) + N_EXPERTS
    P = n_blocks * EXPERT_BLOCK
    buf = jnp.zeros((P, D), x.dtype).at[dest].set(xt[stok])
    block_e = jnp.minimum(jnp.searchsorted(jnp.cumsum(padded), jnp.arange(n_blocks) * EXPERT_BLOCK,
                                           side='right'), N_EXPERTS - 1)

    def run(args):
        xb, e = args
        return _swiglu(xb, w1[e], w3[e], w2[e])

    yb = lax.map(run, (buf.reshape(n_blocks, EXPERT_BLOCK, D), block_e)).reshape(P, D)
    y = jnp.zeros((T, D), x.dtype).at[stok].add(yb[dest] * sg[:, None].astype(x.dtype))
    return y.reshape(B, S, D)

def second_inputs(seed: int = 0) -> dict:
    key = jax.random.key(seed)
    ks = jax.random.split(key, 32)
    f32 = jnp.float32

    def nrm(k, shape, scale):
        return jax.random.normal(k, shape, f32) * scale

    beta = DEEPNORM_BETA
    return {
        "x": nrm(ks[0], (BATCH, SEQ, D_MODEL), 1.0),
        "p": nrm(ks[1], (DEPTH_2, BATCH, SEQ, PLE_DIM), 1.0),
        "positions": jnp.broadcast_to(jnp.arange(SEQ, dtype=jnp.int32), (BATCH, SEQ)),
        "rel_bias_table": nrm(ks[2], (REL_BUCKETS, DIFF_HEADS), 0.5),
        "w_in": nrm(ks[3], (DEPTH_2, D_MODEL, IN_COLS_2), D_MODEL ** -0.5),
        "b_gate": nrm(ks[4], (DEPTH_2, GATE_COLS), 0.02),
        "lambda_q1": nrm(ks[5], (DEPTH_2, DIFF_HEAD_DIM), 0.1),
        "lambda_k1": nrm(ks[6], (DEPTH_2, DIFF_HEAD_DIM), 0.1),
        "lambda_q2": nrm(ks[7], (DEPTH_2, DIFF_HEAD_DIM), 0.1),
        "lambda_k2": nrm(ks[8], (DEPTH_2, DIFF_HEAD_DIM), 0.1),
        "diff_subln_g": 1.0 + nrm(ks[9], (DEPTH_2, DIFF_V_DIM), 0.02),
        "mla_q_norm_g": 1.0 + nrm(ks[10], (DEPTH_2, MLA_Q_RANK), 0.02),
        "w_uq": nrm(ks[11], (DEPTH_2, MLA_Q_RANK, MLA_HEADS * (MLA_NOPE_DIM + MLA_ROPE_DIM)), MLA_Q_RANK ** -0.5),
        "mla_kv_norm_g": 1.0 + nrm(ks[12], (DEPTH_2, MLA_KV_RANK), 0.02),
        "w_ukv": nrm(ks[13], (DEPTH_2, MLA_KV_RANK, MLA_HEADS * (MLA_NOPE_DIM + MLA_V_DIM)), MLA_KV_RANK ** -0.5),
        "w_branch_diff": nrm(ks[14], (DEPTH_2, DIFF_HEADS * DIFF_V_DIM, D_MODEL), (DIFF_HEADS * DIFF_V_DIM) ** -0.5),
        "w_branch_mla": nrm(ks[15], (DEPTH_2, MLA_HEADS * MLA_V_DIM, D_MODEL), (MLA_HEADS * MLA_V_DIM) ** -0.5),
        "w_out": nrm(ks[16], (DEPTH_2, D_MODEL, D_MODEL), beta * D_MODEL ** -0.5),
        "ln_mix_g": 1.0 + nrm(ks[17], (DEPTH_2, D_MODEL), 0.02),
        "ln_mix_b": nrm(ks[18], (DEPTH_2, D_MODEL), 0.02),
        "dense_w1": nrm(ks[19], (N_DENSE, D_MODEL, DENSE_FF), D_MODEL ** -0.5),
        "dense_w3": nrm(ks[20], (N_DENSE, D_MODEL, DENSE_FF), D_MODEL ** -0.5),
        "dense_w2": nrm(ks[21], (N_DENSE, DENSE_FF, D_MODEL), beta * DENSE_FF ** -0.5),
        "router_w": nrm(ks[22], (N_MOE, D_MODEL, N_EXPERTS), D_MODEL ** -0.5),
        "expert_w1": nrm(ks[23], (N_MOE, N_EXPERTS, D_MODEL, EXPERT_FF), D_MODEL ** -0.5),
        "expert_w3": nrm(ks[24], (N_MOE, N_EXPERTS, D_MODEL, EXPERT_FF), D_MODEL ** -0.5),
        "expert_w2": nrm(ks[25], (N_MOE, N_EXPERTS, EXPERT_FF, D_MODEL), beta * EXPERT_FF ** -0.5),
        "w_ple_gate": nrm(ks[26], (DEPTH_2, D_MODEL, D_MODEL), D_MODEL ** -0.5),
        "w_ple_proj": nrm(ks[27], (DEPTH_2, PLE_DIM, D_MODEL), beta * PLE_DIM ** -0.5),
        "ln_ffn_g": 1.0 + nrm(ks[28], (DEPTH_2, D_MODEL), 0.02),
        "ln_ffn_b": nrm(ks[29], (DEPTH_2, D_MODEL), 0.02),
    }

def second_block(x, p, positions, rel_bias_table, w_in, b_gate, lambda_q1, lambda_k1, lambda_q2, lambda_k2,
              diff_subln_g, mla_q_norm_g, w_uq, mla_kv_norm_g, w_ukv, w_branch_diff, w_branch_mla, w_out,
              ln_mix_g, ln_mix_b, dense_w1, dense_w3, dense_w2, router_w, expert_w1, expert_w3, expert_w2,
              w_ple_gate, w_ple_proj, ln_ffn_g, ln_ffn_b):
    for i in range(DEPTH_2):
        lam_init = 0.8 - 0.6 * math.exp(-0.3 * i)
        y = _mixer(x, positions, rel_bias_table, w_in[i], b_gate[i], lambda_q1[i], lambda_k1[i],
                   lambda_q2[i], lambda_k2[i], lam_init, diff_subln_g[i], mla_q_norm_g[i], w_uq[i],
                   mla_kv_norm_g[i], w_ukv[i], w_branch_diff[i], w_branch_mla[i], w_out[i])
        x = _layernorm(DEEPNORM_ALPHA * x + y, ln_mix_g[i], ln_mix_b[i])
        j = i // 2
        if i % 2 == 0:
            f = _swiglu(x, dense_w1[j], dense_w3[j], dense_w2[j])
        else:
            f = _moe(x, router_w[j], expert_w1[j], expert_w3[j], expert_w2[j])
        e = jax.nn.sigmoid(x @ w_ple_gate[i]) * (p[i] @ w_ple_proj[i])
        x = _layernorm(DEEPNORM_ALPHA * x + f + e, ln_ffn_g[i], ln_ffn_b[i])
    return x


def setup_inputs(seed=0):
    out = dict(first_inputs(seed))
    for name, value in second_inputs(seed + 1).items():
        if name != "x":
            out[name + "_2"] = value
    return out


def reference(
    x, ffn1_norm, ffn1_w_in, ffn1_w_out, mix_norm, w_in, b_gate, rwkv_mu, rwkv_w0, rwkv_w2,
    rwkv_a0, rwkv_a2, rwkv_g2, rwkv_k_k, rwkv_k_a, rwkv_r_k, rwkv_ln_w, rwkv_ln_b, attn_q_norm,
    attn_k_norm, w_proj_rwkv, w_proj_attn, w_out, ffn2_norm, ffn2_w_in, ffn2_w_out, p_2,
    positions_2, rel_bias_table_2, w_in_2, b_gate_2, lambda_q1_2, lambda_k1_2, lambda_q2_2,
    lambda_k2_2, diff_subln_g_2, mla_q_norm_g_2, w_uq_2, mla_kv_norm_g_2, w_ukv_2,
    w_branch_diff_2, w_branch_mla_2, w_out_2, ln_mix_g_2, ln_mix_b_2, dense_w1_2, dense_w3_2,
    dense_w2_2, router_w_2, expert_w1_2, expert_w3_2, expert_w2_2, w_ple_gate_2, w_ple_proj_2,
    ln_ffn_g_2, ln_ffn_b_2,
):
    x = first_block(
        x, ffn1_norm, ffn1_w_in, ffn1_w_out, mix_norm, w_in, b_gate, rwkv_mu, rwkv_w0, rwkv_w2,
        rwkv_a0, rwkv_a2, rwkv_g2, rwkv_k_k, rwkv_k_a, rwkv_r_k, rwkv_ln_w, rwkv_ln_b,
        attn_q_norm, attn_k_norm, w_proj_rwkv, w_proj_attn, w_out, ffn2_norm, ffn2_w_in,
        ffn2_w_out,
    )
    return second_block(
        x, p_2, positions_2, rel_bias_table_2, w_in_2, b_gate_2, lambda_q1_2, lambda_k1_2,
        lambda_q2_2, lambda_k2_2, diff_subln_g_2, mla_q_norm_g_2, w_uq_2, mla_kv_norm_g_2,
        w_ukv_2, w_branch_diff_2, w_branch_mla_2, w_out_2, ln_mix_g_2, ln_mix_b_2, dense_w1_2,
        dense_w3_2, dense_w2_2, router_w_2, expert_w1_2, expert_w3_2, expert_w2_2, w_ple_gate_2,
        w_ple_proj_2, ln_ffn_g_2, ln_ffn_b_2,
    )


_drawn_inputs = setup_inputs


def setup_inputs(seed=0):
    import zlib

    import numpy as np

    out = dict(_drawn_inputs(seed))
    spreads = {}
    factors = {'b_gate': 3.747,
     'rwkv_w2': 8.0,
     'rwkv_a0': 3.787,
     'rwkv_ln_b': 8.0,
     'attn_q_norm': 6.169,
     'attn_k_norm': 6.734,
     'b_gate_2': 8.0,
     'lambda_q2_2': 8.0,
     'diff_subln_g_2': 5.466,
     'mla_q_norm_g_2': 8.0,
     'mla_kv_norm_g_2': 8.0}
    for name, (base, spread) in spreads.items():
        noise = np.random.default_rng([zlib.crc32(name.encode()), seed]).standard_normal(out[name].shape)
        drawn = base * np.exp(spread * noise) if base else spread * noise
        out[name] = __import__('jax').numpy.asarray(drawn.astype(out[name].dtype))
    for name, factor in factors.items():
        out[name] = (out[name] * factor).astype(out[name].dtype)
    return out
```

```python
import math
from contextlib import ExitStack

import numpy as np

import concourse.bass as bass
from concourse import mybir

F32 = mybir.dt.float32
I32 = mybir.dt.int32
ALU = mybir.AluOpType
ACT = mybir.ActivationFunctionType
AX = mybir.AxisListType.X

P = 128
S = 256
T = S // P
D = 1024
KD = D // P
HD = 64
F_DENSE = 2816
F_EXPERT = 3584
UNIT = 256
U_DENSE = F_DENSE // UNIT
U_EXPERT = F_EXPERT // UNIT
N_EXPERTS = 8
PLACES = 96
MAX_PASSES = -(-S // PLACES)
SLOTS = 4
SLOT = 4096
CHUNK = 64
N_CHUNKS = S // CHUNK
RHEADS = 16
AHEADS = 12
ATILES = AHEADS // 2
DHEADS = 8
MHEADS = 8
RMS_EPS = 1e-6
GN_EPS = 64e-5
EPS = 1e-5
NEG = -1e30
DEPTH_2 = 2
ALPHA = (2.0 * DEPTH_2) ** 0.25
LAM = math.exp(-0.5)
MLA_SCALE = 96 ** -0.5
NQ, NKV = 3, 2
REL_BUCKETS = 32
KEYS = 3 * P

COLS = {}


def _columns():
    at = 0
    for name, n in [
        ("ffn1_norm", 8), ("mix_norm", 8), ("ffn2_norm", 8), ("b_gate", 16), ("mu", 24), ("mu_wa", 1),
        ("mu_g", 1), ("mu_g2", 1), ("w0", 8), ("a0", 8), ("k_k", 8), ("k_a", 8), ("r_k", 8), ("ln_w", 8), ("ln_b", 8),
        ("q_norm", 1), ("k_norm", 1),
        ("b_gate0", 16), ("subln0", 1), ("mlaq0", 3), ("mlakv0", 2),
        ("b_gate1", 16), ("subln1", 1), ("mlaq1", 3), ("mlakv1", 2),
    ]:
        COLS[name] = at
        at += n
    return at


N_COLS = _columns()

HALF = REL_BUCKETS // 2
THRESHOLDS = list(range(1, HALF + 1)) + [
    math.ceil(HALF * (128 / HALF) ** (j / (REL_BUCKETS - HALF)) - 1e-9) for j in range(1, REL_BUCKETS - HALF)]

STEPS = -(-len(THRESHOLDS) // U_DENSE)

CONST = {}


def constants():
    i = np.arange(P)
    row, col = i[:, None], i[None, :]
    sets = {}

    def add(which, name, a):
        parts = sets.setdefault(which, [])
        CONST[name] = which, sum(p.shape[1] for p in parts)
        parts.append(np.broadcast_to(np.asarray(a, np.float32), (P, np.shape(a)[1])))

    add("always", "ident", row == col)
    add("always", "ones", np.ones((P, P)))
    add("always", "headones", row // HD == col // HD)
    half = 16
    freq = np.zeros((P, 2), np.float32)
    freq[64:96, 0] = np.tile((10000.0 ** (-np.arange(half, dtype=np.float32) / np.float32(half))).astype(np.float32), 2)
    freq[64:80, 1] = -1.0
    freq[80:96, 1] = 1.0
    add("always", "freq", freq)
    add("always", "order", 8.0 - np.arange(8.0)[None, :])
    add("carry", "carry", (np.arange(S) % CHUNK != 0)[None, :])
    same = row // CHUNK == col // CHUNK
    add("rwkv", "before", same & (row < col))
    add("rwkv", "upto", same & (row <= col))
    add("rwkv", "eye64", (row % HD) == np.arange(HD)[None, :])
    add("rwkv", "level0", (row // 2 == col // 2) & (row > col))
    for l in range(6):
        b = 1 << l
        add("rwkv", f"levelT{l}", (row // (2 * b) == col // (2 * b)) & (row % (2 * b) < b) & (col % (2 * b) >= b))
    q = np.concatenate([np.tile(row, (1, P)), np.tile(row + P, (1, S))], 1)
    k = np.concatenate([np.tile(col, (P, 1)), np.tile(np.arange(S)[None, :], (P, 1))], 1)
    for g, (window, dilation) in enumerate(((128, 1), (512, 4), (2048, 16))):
        ok = (k <= q) & ((q - k) % dilation == 0) & (q - k <= window)
        add("dilated", f"mask{g}", np.where(ok, 0.0, NEG))
    add("causal", "causal", np.where(k <= q, 0.0, NEG))
    add("causal", "thresholds", np.array(THRESHOLDS + [1e9] * (STEPS * U_DENSE - len(THRESHOLDS)))[None, :])
    add("causal", "tokens_upto", row <= col)
    add("causal", "places", np.arange(PLACES)[None, :])
    return {which: np.ascontiguousarray(np.concatenate(parts, 1)) for which, parts in sets.items()}


CONSTANTS = constants()


class Chain:

    def __init__(self, eng, sem):
        self.eng, self.sem, self.n, self.seen = eng, sem, 0, 0

    def add(self, ins):
        ins.then_inc(self.sem, 1)
        self.n += 1

    def fence(self):
        if self.n > self.seen:
            self.eng.wait_ge(self.sem, self.n)
            self.seen = self.n

    def step(self, ins):
        self.add(ins)
        self.fence()


def two_blocks(nc, dram, out):
    with ExitStack() as ctx:
        def sb(name, shape, dt=F32):
            return ctx.enter_context(nc.sbuf_tensor(name, shape, dt))

        sem = {}

        def named(name):
            if name not in sem:
                sem[name] = ctx.enter_context(nc.semaphore(name))
            return sem[name]

        slot = [sb(f"slot{i}", [P, SLOT]) for i in range(SLOTS)]
        x_tm = sb("x_tm", [P, T, D])
        h_cm = sb("h_cm", [P, KD, S])
        xn = sb("xn", [P, T, D])
        consts = sb("consts", [P, CONSTANTS["always"].shape[1]])
        turn_consts = sb("turn_consts", [P, CONSTANTS["rwkv"].shape[1]])
        cols = sb("cols", [P, N_COLS])
        stat = sb("stat", [P, 64])
        ff = sb("ff", [P, 4, 512])
        arena = sb("arena", [P, 13 * 2048])
        silu = [ff[:, i, :] for i in range(2)]
        hidden = [ff[:, 2 + i, :].rearrange("p (k s) -> p k s", k=2) for i in range(2)]

        def block8(i, n=1):
            return arena[:, i * 2048:(i + n) * 2048]

        def cm(i):
            return block8(i).rearrange("p (k s) -> p k s", s=S)

        def const(name, n):
            which, at = CONST[name]
            return (consts if which == "always" else turn_consts)[:, at:at + n]

        def col(name, i=0, n=1):
            return cols[:, COLS[name] + i:COLS[name] + i + n]

        ident, ones, headones = const("ident", P), const("ones", P), const("headones", P)

        PS = [ctx.enter_context(nc.psum_tensor(f"bank{i}", [P, 512], F32)) for i in range(8)]
        psum_full = [named(f"psum_full{i}") for i in range(8)]
        psum_free = [named(f"psum_free{i}") for i in range(8)]
        slot_loaded = [named(f"slot_loaded{i}") for i in range(SLOTS)]
        gate_ready, up_ready, silu_ready, hidden_ready, down_done = (
            named(n) for n in ("gate_ready", "up_ready", "silu_ready", "hidden_ready", "down_done"))

        stream = []

        def slabs(name):
            stream.extend(((name, i), dram[name][i], dram[name].shape[2]) for i in range(dram[name].shape[0]))

        stream.append(("ffn", "ffn1", U_DENSE))
        for name in ("w_in_a", "w_in_rkv", "w_in_gates", "w_in_v0", "w_in_v1", "w_in_qk"):
            slabs(name)
        slabs("w_proj_rwkv")
        slabs("w_proj_attn")
        slabs("w_out")
        stream.append(("ffn", "ffn2", U_DENSE))
        for l in range(DEPTH_2):
            for name in ("lat_", "latr_", "dv_", "dqk_", "g2_", "uq_", "ukv_", "bdiff_", "bmla_", "out2_"):
                slabs(f"{name}{l}")
            if l == 0:
                slabs("plegate_0")
                slabs("pleproj_0")
                stream.append(("ffn", "dense", U_DENSE))
            else:
                slabs("plegate_1")
                slabs("pleproj_1")
                stream.append(("experts", "experts", N_EXPERTS * U_EXPERT))
        first_load, unit_base = {}, {}
        n_loads = n_units = 0
        for key, *rest in stream:
            if key in ("ffn", "experts"):
                first_load[rest[0]], unit_base[rest[0]] = n_loads, n_units
                n_loads += 2 * rest[1]
                n_units += rest[1]
            else:
                first_load[key] = n_loads
                n_loads += 1
        last_reader = {}

        job, turns, fillings = {}, [0] * 8, [0] * 8

        def fill(pe, key, bank):
            if turns[bank]:
                pe.wait_ge(psum_free[bank], turns[bank])
            turns[bank] += 1
            job[key] = bank, turns[bank], fillings[bank] + 1
            return PS[bank]

        def filled(ins, key):
            ins.then_inc(psum_full[job[key][0]], 1)
            fillings[job[key][0]] += 1

        def full(eng, key):
            eng.wait_ge(psum_full[job[key][0]], job[key][2])
            return PS[job[key][0]]

        def free(ins, key):
            ins.then_inc(psum_free[job[key][0]], 1)

        def drained(eng, key):
            eng.wait_ge(psum_free[job[key][0]], job[key][1])

        def slab(pe, key):
            load = first_load[key]
            pe.wait_ge(slot_loaded[load % SLOTS], 16 * (load // SLOTS + 1))
            return slot[load % SLOTS]

        def released(key, by):
            last_reader[first_load[key]] = psum_full[job[by][0]], job[by][2]

        def product_cm(pe, key, bank, w, width, tiles, rhs, ks):
            ps = fill(pe, key, bank)
            for j, (c0, m) in enumerate(tiles):
                for k in range(ks):
                    ins = pe.matmul(ps[0:m, j * S:(j + 1) * S], w[:, k * width + c0:k * width + c0 + m],
                                    rhs[:, k, :], start=k == 0, stop=k == ks - 1)
            filled(ins, key)

        def product_tm(pe, key, bank, w, width, c0, n, lhs, ks, t, start=True, stop=True):
            ps = fill(pe, key, bank) if start else PS[bank]
            for k in range(ks):
                ins = pe.matmul(ps[:, 0:n], lhs[:, k, t * P:(t + 1) * P],
                                w[:, k * width + c0:k * width + c0 + n],
                                start=start and k == 0, stop=stop and k == ks - 1)
            if stop:
                filled(ins, key)

        NORMS = {"ffn1": ("ffn1_norm", 0), "mix": ("mix_norm", 1), "ffn2": ("ffn2_norm", 2)}

        def act_norm(act, ch, name, x_done):
            gain, n = NORMS[name]
            x_done(act)
            for t in range(T):
                ins = act.activation(xn[:, t, :], x_tm[:, t, :], ACT.Square, accum_out=stat[:, t:t + 1])
            ins.then_inc(named("sumsq_ready"), 1)
            act.wait_ge(named("meansq_ready"), n + 1)
            act.activation(stat[:, 4:6], stat[:, 2:4], ACT.Sqrt).then_inc(named("rms_ready"), 1)
            act_turned(act, ("norm", name), lambda k: col(gain, k))

        def act_turned(act, key, scale):
            for b in (0, 2):
                ps = full(act, (key, b))
                for kk in range(2):
                    ins = act.mul(h_cm[:, 2 * b + kk, :], ps[:, kk * S:(kk + 1) * S], scale(2 * b + kk)) if scale \
                        else act.copy(h_cm[:, 2 * b + kk, :], ps[:, kk * S:(kk + 1) * S])
                free(ins, (key, b))

        def dve_turned(dve, key, scale):
            for b in (1, 3):
                ps = full(dve, (key, b))
                for kk in range(2):
                    src = ps[:, kk * S:(kk + 1) * S]
                    if scale:
                        ins = nc.vector.tensor_scalar(h_cm[:, 2 * b + kk, :], src, scale(2 * b + kk), None, ALU.mult)
                    else:
                        ins = nc.vector.tensor_copy(h_cm[:, 2 * b + kk, :], src)
                free(ins, (key, b))

        def dve_norm(dve, ch, name):
            gain, n = NORMS[name]
            dve.wait_ge(named("sumsq_ready"), n + 1)
            nc.vector.tensor_scalar(stat[:, 2:4], stat[:, 0:2], 1.0 / D, RMS_EPS, ALU.mult, ALU.add
                                    ).then_inc(named("meansq_ready"), 1)
            dve.wait_ge(named("rms_ready"), n + 1)
            ch.step(nc.vector.reciprocal(stat[:, 6:8], stat[:, 4:6]))
            for t in range(T):
                nc.vector.tensor_scalar(xn[:, t, :], x_tm[:, t, :], stat[:, 6 + t:7 + t], None, ALU.mult
                                        ).then_inc(named("xn_ready"), 1)
            dve_turned(dve, ("norm", name), lambda k: col(gain, k))

        def pe_turn(pe, key, src):
            for b in range(4):
                ps = fill(pe, (key, b), b)
                for kk in range(2):
                    for t in range(T):
                        k = 2 * b + kk
                        ins = pe.transpose(ps[:, kk * S + t * P:kk * S + (t + 1) * P],
                                           src[:, t, k * P:(k + 1) * P], ident)
                filled(ins, (key, b))

        def pe_norm(pe, name):
            pe.wait_ge(named("xn_ready"), T * (NORMS[name][1] + 1))
            pe_turn(pe, ("norm", name), xn)

        def h_written(eng, key):
            for b in range(4):
                drained(eng, (key, b))

        def pe_up(pe, par, n, loads, s, peeled):
            pe.wait_ge(slot_loaded[s], 16 * loads)
            if not peeled:
                pe.wait_ge(silu_ready, n - 1)
            for half, bank, ready in ((0, PS[par], gate_ready), (1, PS[2 + par], up_ready)):
                if half and not peeled:
                    pe.wait_ge(hidden_ready, n - 1)
                for m in range(2):
                    for k in range(KD):
                        c0 = k * 512 + half * UNIT + m * P
                        ins = pe.matmul(bank[:, m * S:(m + 1) * S], slot[s][:, c0:c0 + P], h_cm[:, k, :],
                                        start=k == 0, stop=k == KD - 1)
                ins.then_inc(ready, 1)

        def pe_down(pe, par, n, loads, s, start=False, stop=False):
            pe.wait_ge(slot_loaded[s], 16 * loads)
            pe.wait_ge(hidden_ready, n + 1)
            for t in range(T):
                for half in range(2):
                    for kk in range(2):
                        ins = pe.matmul(PS[4 + 2 * t + half][:, :], hidden[par][:, kk, t * P:(t + 1) * P],
                                        slot[s][:, kk * D + half * 512:kk * D + half * 512 + 512],
                                        start=start and kk == 0, stop=stop and kk == 1, skip_group_check=True)
            ins.then_inc(down_done, 1)

        def ffn_open(pe):
            for b in range(4):
                if turns[b]:
                    pe.wait_ge(psum_free[b], turns[b])

        def pe_ffn(pe, name):
            L, n0 = first_load[name], unit_base[name]
            ffn_open(pe)
            for i in range(4):
                fill(pe, (name, i), 4 + i)

            def up(u, peeled=False):
                i, j = u
                at = L + 2 * j
                pe_up(pe, (n0 + j) % 2, n0 + j + 2 * i, at // SLOTS + 1 + i, at % SLOTS, peeled)

            def down(u, **kw):
                i, j = u
                at = L + 2 * j + 1
                pe_down(pe, (n0 + j) % 2, n0 + j + 2 * i, at // SLOTS + 1 + i, at % SLOTS, **kw)

            up((0, 0), peeled=True)
            up((0, 1), peeled=True)
            down((0, 0), start=True)
            pairs = (U_DENSE - 3) // 2
            with pe.Fori(0, pairs) as i:
                up((i, 2))
                down((i, 1))
                up((i, 3))
                down((i, 2))
            assert U_DENSE == 2 * pairs + 3
            up((pairs, 2))
            down((pairs, 1))
            down((pairs, 2), stop=True)

        def full_sum(eng, name):
            eng.wait_ge(down_done, unit_base[name] + U_DENSE)

        def act_ffn(act, name):
            n0 = unit_base[name]
            count = U_DENSE

            def unit(par, n, peeled):
                act.wait_ge(gate_ready, n + 1)
                if not peeled:
                    act.wait_ge(hidden_ready, n - 1)
                act.activation(silu[par], PS[par][:, :], ACT.Silu).then_inc(silu_ready, 1)

            unit(n0 % 2, n0, True)
            unit((n0 + 1) % 2, n0 + 1, True)
            with act.Fori(1, count // 2) as i:
                unit(n0 % 2, i * 2 + n0, False)
                unit((n0 + 1) % 2, i * 2 + n0 + 1, False)
            if count % 2:
                unit((n0 + count - 1) % 2, n0 + count - 1, False)

        def dve_unit(dve, par, n, peeled):
            dve.wait_ge(up_ready, n + 1)
            dve.wait_ge(silu_ready, n + 1)
            if not peeled:
                dve.wait_ge(down_done, n - 1)
            nc.vector.tensor_tensor(ff[:, 2 + par, :], silu[par], PS[2 + par][:, :], ALU.mult
                                    ).then_inc(hidden_ready, 1)

        def dve_ffn(dve, name, beside=lambda u: None):
            n0 = unit_base[name]
            for j in range(2):
                dve_unit(dve, (n0 + j) % 2, n0 + j, True)
                beside(j)
            with dve.Fori(1, U_DENSE // 2) as i:
                for j in range(2):
                    dve_unit(dve, (n0 + j) % 2, i * 2 + n0 + j, False)
                    beside(i * 2 + j)
            dve_unit(dve, (n0 + U_DENSE - 1) % 2, n0 + U_DENSE - 1, False)
            beside(U_DENSE - 1)

        def sp_ffn(sp, name, source):
            L, n0 = first_load[name], unit_base[name]
            count = U_DENSE

            def unit(j, index, n, peeled):
                for part, (c0, c1, used) in enumerate(((0, 4096, up_ready), (4096, 6144, down_done))):
                    load = L + 2 * j + part
                    if not peeled:
                        sp.wait_ge(used, n - 1)
                    elif load >= SLOTS:
                        sp.wait_ge(*last_reader[load - SLOTS])
                    sp.dma_start(slot[load % SLOTS][:, 0:c1 - c0], source[index][:, c0:c1]
                                 ).then_inc(slot_loaded[load % SLOTS], 16)

            unit(0, 0, n0, True)
            unit(1, 1, n0 + 1, True)
            with sp.Fori(1, count // 2) as i:
                unit(0, i * 2, i * 2 + n0, False)
                unit(1, i * 2 + 1, i * 2 + n0 + 1, False)
            if count % 2:
                unit(0, count - 1, n0 + count - 1, False)
            for u in (count - 2, count - 1):
                last_reader[L + 2 * u] = up_ready, n0 + u + 1
                last_reader[L + 2 * u + 1] = down_done, n0 + u + 1

        def dve_add_half(dve, name):
            full_sum(dve, name)
            for i in range(4):
                t, half = divmod(i, 2)
                part = x_tm[:, t, half * 512:half * 512 + 512]
                free(nc.vector.scalar_tensor_tensor(part, PS[4 + i][:, :], 0.5, part, ALU.mult, ALU.add), (name, i))

        def x_after(name):
            def wait(eng):
                for i in range(4):
                    drained(eng, (name, i))
            return wait

        def spread(ap, n):
            return ap.unsqueeze(ap.ndim).broadcast_to(list(ap.shape) + [n])

        def times(ap, n, at=1):
            shape = list(ap.shape)
            return ap.unsqueeze(at).broadcast_to(shape[:at] + [n] + shape[at:])

        rotation = [0]

        def next_bank():
            rotation[0] = (rotation[0] + 1) % 8
            return rotation[0]

        R, K, V, DEC, A, G, CUM, KK, TMP, BONUS, EC = (cm(i) for i in range(11))
        gates = arena[:, 11 * 2048:13 * 2048].rearrange("p (k s) -> p k s", s=S)
        lora_wa = arena[:, 10 * 2048:10 * 2048 + 1024]
        lora_g = block8(9)
        lora_in = block8(8)[:, 0:768].rearrange("p (k s) -> p k s", s=S)
        CARRY = block8(8)[:, 768:1024]
        raw = [xn[:, :, :].rearrange("p t d -> p (t d)")[:, i * 514:(i + 1) * 514].rearrange("p (k s) -> p k s", k=2)
               for i in range(2)]
        shift_tmp = xn[:, :, :].rearrange("p t d -> p (t d)")[:, 1028:1540].rearrange("p (k s) -> p k s", k=2)

        def tm(i):
            return block8(i).rearrange("p (t d) -> p t d", t=T)

        A_TM, B_TM, K_TM, V_TM = tm(4), tm(6), tm(8), tm(10)
        TM_SOURCES = (("a", DEC, A_TM), ("b", KK, B_TM), ("k", K, K_TM), ("v", V, V_TM))
        xflat = xn[:, :, :].rearrange("p t d -> p (t d)")
        LT = block8(2)[:, 0:1024].rearrange("p (h m i s) -> p h m i s", h=2, m=2, i=2)
        MT = block8(2)[:, 1024:2048].rearrange("p (h m i s) -> p h m i s", h=2, m=2, i=2)
        TI, TT, AM, X1 = (xflat[:, i * 512:(i + 1) * 512].rearrange("p (h i s) -> p h i s", h=2, i=2) for i in range(4))
        XV = ff[:, 0, 0:256].rearrange("p (h i d) -> p h i d", h=2, i=2)
        WU = ff[:, 1, :].rearrange("p (h i d) -> p h i d", h=2, i=2)
        decay_end = ff[:, 2, 0:32].rearrange("p (k c) -> p k c", c=N_CHUNKS)
        STATE = block8(4).rearrange("p (c k d) -> p c k d", c=4, k=KD)
        state_tmp = block8(6)[:, 0:512].rearrange("p (k d) -> p k d", k=KD)
        GROUPS = [(t, g) for t in range(T) for g in range(4)]
        HEADS = [(p, i) for p in range(2) for i in range(2)]
        SHIFTS = [(("lora", 0), [("mu_wa", 0, lora_in[:, 0, :], P), ("mu_g", 0, lora_in[:, 1, :], P)]),
                  (("lora", 1), [("mu_g2", 0, lora_in[0:32, 2, :], 32)])]
        for tile in range(0, 24, 2):
            SHIFTS.append((("rkv", tile), [("mu", tile + j, (R, K, V)[tile // 8][:, tile % 8 + j, :], P)
                                           for j in range(2)]))

        def pe_rwkv_in(pe):
            h_written(pe, ("norm", "mix"))
            w = slab(pe, ("w_in_a", 0))
            product_cm(pe, ("lora", 0), next_bank(), w, 288, [(0, P), (P, P)], h_cm, KD)
            product_cm(pe, ("lora", 1), next_bank(), w, 288, [(2 * P, 32)], h_cm, KD)
            released(("w_in_a", 0), ("lora", 1))
            for s in range(6):
                w = slab(pe, ("w_in_rkv", s))
                for j in range(2):
                    product_cm(pe, ("rkv", 4 * s + 2 * j), next_bank(), w, 512,
                               [(2 * j * P, P), ((2 * j + 1) * P, P)], h_cm, KD)
                released(("w_in_rkv", s), ("rkv", 4 * s + 2))
                if s == 1:
                    pe.wait_ge(named("lora_act"), 3)
                    pe.wait_ge(named("lora_loaded"), 48)
                    for kind, lo in (("w", 0), ("a", 64)):
                        for b in range(4):
                            ps = fill(pe, (kind, b), next_bank())
                            for j in range(2):
                                c0 = (2 * b + j) * P
                                ins = pe.matmul(ps[:, j * S:(j + 1) * S], lora_wa[lo:lo + 64, c0:c0 + P],
                                                lora_in[lo:lo + 64, 0, :], start=True, stop=True)
                            filled(ins, (kind, b))
                    for b in range(4):
                        ps = fill(pe, ("g", b), next_bank())
                        for j in range(2):
                            c0 = (2 * b + j) * P
                            pe.matmul(ps[:, j * S:(j + 1) * S], lora_g[:, c0:c0 + P], lora_in[:, 1, :],
                                      start=True, stop=False)
                            ins = pe.matmul(ps[:, j * S:(j + 1) * S], lora_g[0:32, D + c0:D + c0 + P],
                                            lora_in[0:32, 2, :], start=False, stop=True)
                        filled(ins, ("g", b))
            for s in range(4):
                w = slab(pe, ("w_in_gates", s))
                for j in range(2):
                    product_cm(pe, ("gate", 4 * s + 2 * j), next_bank(), w, 512,
                               [(2 * j * P, P), ((2 * j + 1) * P, P)], h_cm, KD)
                released(("w_in_gates", s), ("gate", 4 * s + 2))

        def act_rwkv_in(act, ch):
            act.wait_ge(named("shift_zero"), 1)
            for n, (key, parts) in enumerate(SHIFTS):
                if n >= 2:
                    act.wait_ge(named("shifted"), n - 1)
                ps = full(act, key)
                m = parts[0][3]
                ins = act.copy(raw[n % 2][0:m, 0:len(parts), 1:S + 1],
                               ps[0:m, 0:len(parts) * S].rearrange("p (k s) -> p k s", s=S))
                free(ins, key)
                if n == 2:
                    act.wait_ge(named("shifted"), 2)
                    act.activation(lora_in[0:64, 0, :], lora_in[0:64, 0, :], ACT.Tanh).then_inc(named("lora_act"), 1)
                    act.activation(lora_in[:, 1, :], lora_in[:, 1, :], ACT.Sigmoid).then_inc(named("lora_act"), 1)
                    act.activation(lora_in[0:32, 2, :], lora_in[0:32, 2, :], ACT.Sigmoid).then_inc(named("lora_act"), 1)
                if n == 5:
                    for kind, name, dst in (("w", "w0", DEC), ("a", "a0", A)):
                        for b in range(4):
                            ps = full(act, (kind, b))
                            for j in range(2):
                                ins = act.activation(dst[:, 2 * b + j, :], ps[:, j * S:(j + 1) * S], ACT.Sigmoid,
                                                     bias=col(name, 2 * b + j))
                            free(ins, (kind, b))
                    for b in range(4):
                        ps = full(act, ("g", b))
                        free(act.copy(G[:, 2 * b:2 * b + 2, :], ps[:, :].rearrange("p (k s) -> p k s", s=S)), ("g", b))
            for tile in range(0, 16, 2):
                if tile == 4:
                    act_decays(act)
                ps = full(act, ("gate", tile))
                for j in range(2):
                    ins = act.activation(gates[:, tile + j, :], ps[:, j * S:(j + 1) * S], ACT.Sigmoid,
                                         bias=col("b_gate", tile + j))
                free(ins, ("gate", tile))

        def act_decays(act):
            act.wait_ge(named("cum_ready"), 1)
            act.activation(EC, CUM, ACT.Exp, scale=-LAM)
            act.activation(DEC, DEC, ACT.Exp, scale=-LAM)
            act.activation(CUM, CUM, ACT.Exp, scale=LAM).then_inc(named("decays_ready"), 1)

        def dve_rwkv_in(dve, ch):
            h_written(dve, ("norm", "mix"))
            for i in range(2):
                ins = nc.vector.memset(raw[i][:, :, 0:1], 0.0)
                ch.add(ins)
            ch.fence()
            dve.sem_inc(named("shift_zero"), 1)
            for n, (key, parts) in enumerate(SHIFTS):
                drained(dve, key)
                m, k = parts[0][3], len(parts)
                if n:
                    dve.wait_ge(named("shifted"), n)
                ch.step(nc.vector.tensor_tensor(shift_tmp[0:m, 0:k, :], raw[n % 2][0:m, 0:k, 0:S],
                                                raw[n % 2][0:m, 0:k, 1:S + 1], ALU.subtract))
                for j, (mu, c, dst, _) in enumerate(parts):
                    ins = nc.vector.scalar_tensor_tensor(dst, shift_tmp[0:m, j, :], col(mu, c)[0:m, :],
                                                         raw[n % 2][0:m, j, 1:S + 1], ALU.mult, ALU.add)
                ins.then_inc(named("shifted"), 1)
            dve.wait_ge(named("shifted"), len(SHIFTS))
            for b in range(4):
                drained(dve, ("w", b))
            for k in range(KD):
                ch.add(nc.vector.tensor_tensor_scan(CUM[:, k, :], CARRY, DEC[:, k, :], 0.0,
                                                    ALU.mult, ALU.add))
            ch.fence()
            nc.vector.tensor_tensor(DEC, CUM, DEC, ALU.subtract).then_inc(named("cum_ready"), 1)
            ch.step(nc.vector.tensor_tensor(KK, K, spread(col("k_k", 0, 8), S), ALU.mult))
            for b in range(4):
                drained(dve, ("g", b))
            nc.vector.tensor_tensor(TMP, KK, KK, ALU.mult).then_inc(named("kk_squared"), 1)
            for b in range(4):
                drained(dve, ("kks", b))
            ch.step(nc.vector.tensor_scalar(TMP, TMP, 1e-12, None, ALU.max))
            ch.step(nc.vector.reciprocal(TMP, TMP))
            ch.step(nc.vector.tensor_tensor(KK, KK, TMP, ALU.mult))
            for b in range(4):
                drained(dve, ("a", b))
            ch.step(nc.vector.scalar_tensor_tensor(TMP, A, 1.0, spread(col("k_a", 0, 8), S), ALU.subtract, ALU.mult))
            ch.step(nc.vector.scalar_tensor_tensor(K, TMP, 1.0, K, ALU.add, ALU.mult))
            ch.step(nc.vector.tensor_tensor(TMP, R, K, ALU.mult))
            nc.vector.tensor_tensor(TMP, TMP, spread(col("r_k", 0, 8), S), ALU.mult).then_inc(named("rk_ready"), 1)
            dve.wait_ge(named("decays_ready"), 1)
            ch.step(nc.vector.scalar_tensor_tensor(DEC, KK, -1.0, DEC, ALU.mult, ALU.mult))
            ch.step(nc.vector.tensor_tensor(KK, KK, A, ALU.mult))
            ch.step(nc.vector.tensor_tensor(KK, KK, CUM, ALU.mult))
            ch.add(nc.vector.tensor_tensor(K, K, CUM, ALU.mult))
            ch.add(nc.vector.tensor_tensor(R, R, EC, ALU.mult))
            for b in range(4):
                ps = full(dve, ("bonus", b))
                free(nc.vector.tensor_tensor(BONUS[:, 2 * b:2 * b + 2, :], ps[:, :].rearrange("p (k s) -> p k s", s=S),
                                             V[:, 2 * b:2 * b + 2, :], ALU.mult), ("bonus", b))
            nc.vector.tensor_copy(decay_end, EC[:, :, CHUNK - 1::CHUNK]).then_inc(named("scaled"), 1)

        def pe_rwkv_chunks(pe):
            pe.wait_ge(named("kk_squared"), 1)
            for b in range(4):
                ps = fill(pe, ("kks", b), next_bank())
                filled(pe.matmul(ps[:, :], headones, TMP[:, 2 * b:2 * b + 2, :], start=True, stop=True), ("kks", b))
            pe.wait_ge(named("rk_ready"), 1)
            for b in range(4):
                ps = fill(pe, ("bonus", b), next_bank())
                filled(pe.matmul(ps[:, :], headones, TMP[:, 2 * b:2 * b + 2, :], start=True, stop=True), ("bonus", b))
            pe.wait_ge(named("scaled"), 1)
            for name, src, _ in TM_SOURCES:
                for t in range(T):
                    for half in range(2):
                        key = ("tm", name, t, half)
                        ps = fill(pe, key, next_bank())
                        for j in range(4):
                            ins = pe.transpose(ps[:, j * P:(j + 1) * P], src[:, 4 * half + j, t * P:(t + 1) * P], ident)
                        filled(ins, key)
            for name, _, _ in TM_SOURCES:
                for t in range(T):
                    for half in range(2):
                        drained(pe, ("tm", name, t, half))
            levels = 0
            for n, (t, g) in enumerate(GROUPS):
                tok = slice(t * P, (t + 1) * P)

                def rows(src, p, i):
                    return src[64 * p:64 * p + 64, 2 * g + i, tok]

                def heads(src, p, i, lo=0, hi=P):
                    c0 = (2 * g + i) * P + 64 * p
                    return src[lo:hi, t, c0:c0 + HD]

                for p in range(2):
                    for key, pairs in ((("LT", n, p), ((KK, DEC), (K, DEC))), (("MT", n, p), ((KK, R), (K, R))),
                                       (("LB", n, p), ((DEC, KK),))):
                        ps = fill(pe, key, next_bank())
                        for m, (left, right) in enumerate(pairs):
                            for i in range(2):
                                c0 = (2 * m + i) * P
                                ins = pe.matmul(ps[:, c0:c0 + P], rows(left, p, i), rows(right, p, i), start=True, stop=True)
                        filled(ins, key)
                drained(pe, ("LT", n, 0))
                drained(pe, ("LT", n, 1))
                ps = fill(pe, ("XV", n), next_bank())
                for h, (p, i) in enumerate(HEADS):
                    ins = pe.matmul(ps[:, h * HD:(h + 1) * HD], LT[:, p, 1, i, :], heads(V_TM, p, i), start=True, stop=True)
                filled(ins, ("XV", n))
                for l in range(1, 6):
                    pe.wait_ge(named("between"), levels + 1)
                    levels += 1
                    ps = fill(pe, ("X1", n, l), next_bank())
                    for h, (p, i) in enumerate(HEADS):
                        ins = pe.matmul(ps[:, h * P:(h + 1) * P], AM[:, p, i, :], TI[:, p, i, :], start=True, stop=True)
                    filled(ins, ("X1", n, l))
                    drained(pe, ("X1", n, l))
                    for key, left, right in ((("X2", n, l), TT, X1), (("XT", n, l), X1, TT)):
                        if l == 5 and key[0] == "X2":
                            continue
                        ps = fill(pe, key, next_bank())
                        for h, (p, i) in enumerate(HEADS):
                            ins = pe.matmul(ps[:, h * P:(h + 1) * P], left[:, p, i, :], right[:, p, i, :],
                                            start=True, stop=True)
                        filled(ins, key)
                drained(pe, ("XT", n, 5))
                drained(pe, ("XV", n))
                ps = fill(pe, ("WU", n), next_bank())
                for h, (p, i) in enumerate(HEADS):
                    pe.matmul(ps[:, h * P:h * P + HD], TT[:, p, i, :], heads(A_TM, p, i), start=True, stop=True)
                    ins = pe.matmul(ps[:, h * P + HD:(h + 1) * P], TT[:, p, i, :], XV[:, p, i, :], start=True, stop=True)
                filled(ins, ("WU", n))
                drained(pe, ("WU", n))
                drained(pe, ("MT", n, 0))
                drained(pe, ("MT", n, 1))
                ps = fill(pe, ("Q", n), next_bank())
                for p, i in HEADS:
                    ins = pe.matmul(ps[64 * p:64 * p + 64, i * P:(i + 1) * P], WU[:, p, i, 0:HD], MT[:, p, 0, i, :],
                                    start=True, stop=True)
                filled(ins, ("Q", n))
                ps = fill(pe, ("O", n), next_bank())
                for p, i in HEADS:
                    pe.matmul(ps[64 * p:64 * p + 64, i * P:(i + 1) * P], WU[:, p, i, HD:P], MT[:, p, 0, i, :],
                              start=True, stop=False)
                    ins = pe.matmul(ps[64 * p:64 * p + 64, i * P:(i + 1) * P], heads(V_TM, p, i), MT[:, p, 1, i, :],
                                    start=False, stop=True)
                filled(ins, ("O", n))
                for c in range(2):
                    lo, hi = c * CHUNK, (c + 1) * CHUNK
                    ps = fill(pe, ("GH", n, c), next_bank())
                    for p, i in HEADS:
                        o = ps[64 * p:64 * p + 64, i * P:(i + 1) * P]
                        pe.matmul(o[:, 0:HD], WU[lo:hi, p, i, 0:HD], heads(B_TM, p, i, lo, hi), start=True, stop=True)
                        pe.matmul(o[:, HD:P], heads(B_TM, p, i, lo, hi), WU[lo:hi, p, i, HD:P], start=True, stop=False)
                        ins = pe.matmul(o[:, HD:P], heads(K_TM, p, i, lo, hi), heads(V_TM, p, i, lo, hi),
                                        start=False, stop=True)
                    filled(ins, ("GH", n, c))
            for n in range(len(GROUPS)):
                drained(pe, ("Q", n))
                drained(pe, ("GH", n, 1))
            for c in range(1, N_CHUNKS):
                pe.wait_ge(named("state_ready"), c)
                tok = slice(c * CHUNK, (c + 1) * CHUNK)
                for key, left in ((("SG", c), KK), (("SO", c), None)):
                    if key == ("SG", N_CHUNKS - 1):
                        continue
                    ps = fill(pe, key, next_bank())
                    for k in range(KD):
                        for p in range(2):
                            lo = 64 * p
                            o = ps[lo:lo + 64, k * HD:(k + 1) * HD]
                            st = STATE[lo:lo + 64, c, k, :]
                            if left is None:
                                ins = pe.matmul(o, st, R[lo:lo + 64, k, tok], start=True, stop=True)
                            else:
                                ins = pe.matmul(o, KK[lo:lo + 64, k, tok], st, start=True, stop=True)
                    filled(ins, key)
            pe.wait_ge(named("wkv_ready"), 1)
            for key, src in (("gnm", K), ("gnv", CUM)):
                if key == "gnv":
                    pe.wait_ge(named("centred_squared"), 1)
                for b in range(4):
                    ps = fill(pe, (key, b), next_bank())
                    filled(pe.matmul(ps[:, :], headones, src[:, 2 * b:2 * b + 2, :], start=True, stop=True), (key, b))

        def act_rwkv_chunks(act, ch):
            for b in range(4):
                ps = full(act, ("kks", b))
                free(act.activation(TMP[:, 2 * b:2 * b + 2, :], ps[:, :].rearrange("p (k s) -> p k s", s=S), ACT.Sqrt),
                     ("kks", b))
            act.wait_ge(named("scaled"), 1)
            for name, _, dst in TM_SOURCES:
                for t in range(T):
                    ps = full(act, ("tm", name, t, 0))
                    free(act.copy(dst[:, t, 0:512], ps[:, :]), ("tm", name, t, 0))
            for n, (t, g) in enumerate(GROUPS):
                ps = full(act, ("XV", n))
                if n:
                    full(act, ("GH", n - 1, 1))
                free(act.copy(XV.rearrange("p h i d -> p (h i d)"), ps[:, 0:256]), ("XV", n))
                for l in range(1, 6):
                    ps = full(act, ("X1", n, l))
                    free(act.copy(X1.rearrange("p h i s -> p (h i s)"), ps[:, :]), ("X1", n, l))
                ps = full(act, ("WU", n))
                free(act.copy(WU.rearrange("p h i s -> p (h i s)"), ps[:, :]), ("WU", n))
                ps = full(act, ("O", n))
                free(act.copy(K[:, 2 * g:2 * g + 2, t * P:(t + 1) * P],
                              ps[:, 0:256].rearrange("p (i s) -> p i s", i=2)), ("O", n))
            act.wait_ge(named("centred"), 1)
            act.activation(CUM, TMP, ACT.Square).then_inc(named("centred_squared"), 1)
            act.wait_ge(named("gn_var"), 1)
            act.activation(CUM, CUM, ACT.Sqrt).then_inc(named("gn_std"), 1)

        def dve_rwkv_chunks(dve, ch):
            for name, _, dst in TM_SOURCES:
                for t in range(T):
                    ps = full(dve, ("tm", name, t, 1))
                    free(nc.vector.tensor_copy(dst[:, t, 512:1024], ps[:, :]), ("tm", name, t, 1))
            for name, _, dst in TM_SOURCES:
                for t in range(T):
                    drained(dve, ("tm", name, t, 0))
            before, upto = const("before", P), const("upto", P)
            for n, (t, g) in enumerate(GROUPS):
                if n:
                    full(dve, ("GH", n - 1, 1))
                for key, dst, mask in ((("LT", n), LT, before), (("MT", n), MT, upto)):
                    for p in range(2):
                        ps = full(dve, (*key, p))
                        ins = nc.vector.tensor_tensor(dst[:, p, :, :, :].rearrange("p m i s -> p (m i) s"),
                                                      ps[:, :].rearrange("p (m s) -> p m s", s=P), times(mask, 4), ALU.mult)
                        free(ins, (*key, p))
                drained(dve, ("LT", n, 0))
                drained(dve, ("LT", n, 1))
                for p in range(2):
                    ps = full(dve, ("LB", n, p))
                    ins = nc.vector.tensor_tensor(TI[:, p, :, :], ps[:, 0:256].rearrange("p (m s) -> p m s", s=P),
                                                  times(const("level0", P), 2), ALU.mult)
                    free(ins, ("LB", n, p))
                drained(dve, ("LB", n, 0))
                drained(dve, ("LB", n, 1))
                ch.add(nc.vector.tensor_tensor(TT, LT[:, :, 0, :, :], const("levelT0", P).unsqueeze(1).unsqueeze(1)
                                               .broadcast_to([P, 2, 2, P]), ALU.mult))
                ch.add(nc.vector.tensor_tensor(TI, TI, ident.unsqueeze(1).unsqueeze(1).broadcast_to([P, 2, 2, P]), ALU.add))
                ch.fence()
                ch.add(nc.vector.tensor_tensor(TT, TT, ident.unsqueeze(1).unsqueeze(1).broadcast_to([P, 2, 2, P]), ALU.add))
                for l in range(1, 6):
                    if l > 1:
                        for key, dst in ((("X2", n, l - 1), TI), (("XT", n, l - 1), TT)):
                            ps = full(dve, key)
                            flat = dst.rearrange("p h i s -> p (h i s)")
                            free(nc.vector.tensor_tensor(flat, flat, ps[:, :], ALU.add), key)
                    nc.vector.tensor_tensor(AM, LT[:, :, 0, :, :], const(f"levelT{l}", P).unsqueeze(1).unsqueeze(1)
                                            .broadcast_to([P, 2, 2, P]), ALU.mult).then_inc(named("between"), 1)
                ps = full(dve, ("XT", n, 5))
                flat = TT.rearrange("p h i s -> p (h i s)")
                free(nc.vector.tensor_tensor(flat, flat, ps[:, :], ALU.add), ("XT", n, 5))
                ps = full(dve, ("Q", n))
                q = R[:, 2 * g:2 * g + 2, t * P:(t + 1) * P]
                free(nc.vector.tensor_tensor(q, q, ps[:, 0:256].rearrange("p (i s) -> p i s", i=2), ALU.add), ("Q", n))
                for c in range(2):
                    ps = full(dve, ("GH", n, c))
                    gh = ps[:, :].rearrange("p (i m s) -> p i m s", m=2, s=HD)[:, 0:2]
                    tok = slice(t * P + c * CHUNK, t * P + (c + 1) * CHUNK)
                    nc.vector.tensor_tensor(KK[:, 2 * g:2 * g + 2, tok], gh[:, :, 0, :], times(const("eye64", HD), 2), ALU.add)
                    free(nc.vector.tensor_copy(DEC[:, 2 * g:2 * g + 2, tok], gh[:, :, 1, :]), ("GH", n, c))
            drained(dve, ("GH", 7, 1))
            for c in range(N_CHUNKS - 1):
                h = DEC[:, :, c * CHUNK:(c + 1) * CHUNK]
                if c:
                    ps = full(dve, ("SG", c))
                    free(nc.vector.tensor_tensor(state_tmp, ps[:, :].rearrange("p (k d) -> p k d", d=HD), h, ALU.add), ("SG", c))
                    drained(dve, ("SG", c))
                    h = state_tmp
                nc.vector.tensor_tensor(STATE[:, c + 1, :, :], h, spread(decay_end[:, :, c], HD), ALU.mult
                                        ).then_inc(named("state_ready"), 1)
                if c:
                    dve_state_out(dve, c)
            dve_state_out(dve, N_CHUNKS - 1)
            drained(dve, ("SO", N_CHUNKS - 1))
            dve.sem_inc(named("wkv_ready"), 1)
            for b in range(4):
                ps = full(dve, ("gnm", b))
                ins = nc.vector.scalar_tensor_tensor(TMP[:, 2 * b:2 * b + 2, :], ps[:, :].rearrange("p (k s) -> p k s", s=S),
                                                     -1.0 / HD, K[:, 2 * b:2 * b + 2, :], ALU.mult, ALU.add)
                free(ins, ("gnm", b))
                drained(dve, ("gnm", b))
            dve.sem_inc(named("centred"), 1)
            for b in range(4):
                ps = full(dve, ("gnv", b))
                ins = nc.vector.tensor_scalar(CUM[:, 2 * b:2 * b + 2, :], ps[:, :].rearrange("p (k s) -> p k s", s=S),
                                              1.0 / HD, GN_EPS, ALU.mult, ALU.add)
                free(ins, ("gnv", b))
                drained(dve, ("gnv", b))
            dve.sem_inc(named("gn_var"), 1)
            dve.wait_ge(named("gn_std"), 1)
            ch.step(nc.vector.reciprocal(CUM, CUM))
            ch.step(nc.vector.tensor_tensor(TMP, TMP, CUM, ALU.mult))
            ch.step(nc.vector.tensor_tensor(TMP, TMP, spread(col("ln_w", 0, 8), S), ALU.mult))
            ch.step(nc.vector.tensor_tensor(TMP, TMP, spread(col("ln_b", 0, 8), S), ALU.add))
            ch.step(nc.vector.tensor_tensor(TMP, TMP, BONUS, ALU.add))
            nc.vector.tensor_tensor(K, TMP, G, ALU.mult).then_inc(named("y_a_ready"), 1)

        def dve_state_out(dve, c):
            ps = full(dve, ("SO", c))
            o = K[:, :, c * CHUNK:(c + 1) * CHUNK]
            if c == 1:
                for n in range(len(GROUPS)):
                    drained(dve, ("O", n))
            free(nc.vector.tensor_tensor(o, o, ps[:, :].rearrange("p (k d) -> p k d", d=HD), ALU.add), ("SO", c))

        Y_A = K
        QK = arena[:, 2 * 2048:2 * 2048 + 12 * S].rearrange("p (k s) -> p k s", s=S)
        VA = arena[:, 2 * 2048 + 3072:2 * 2048 + 4608].rearrange("p (t d) -> p t d", t=T)
        SQ = arena[:, 5 * 2048:5 * 2048 + 12 * S].rearrange("p (k s) -> p k s", s=S)
        PB = arena[:, 5 * 2048:5 * 2048 + AHEADS * KEYS].rearrange("p (h s) -> p h s", s=KEYS)
        PT = arena[:, 8 * 2048:8 * 2048 + AHEADS * KEYS].rearrange("p (h b s) -> p h b s", b=3, s=P)
        YB = arena[:, 2 * 2048:2 * 2048 + ATILES * S].rearrange("p (k s) -> p k s", s=S)
        MERGED, MTMP = cm(5), cm(6)
        row_max = ff[:, 0, 0:24].rearrange("p (t h) -> p t h", t=T)
        neg_max = ff[:, 0, 24:48].rearrange("p (t h) -> p t h", t=T)
        row_sum = ff[:, 0, 48:72].rearrange("p (t h) -> p t h", t=T)
        row_lse = ff[:, 0, 72:96].rearrange("p (t h) -> p t h", t=T)
        row_w = ff[:, 0, 96:120].rearrange("p (t h) -> p t h", t=T)
        lse_max = ff[:, 0, 120:128].rearrange("p (t h) -> p t h", t=T)
        w_sum = ff[:, 0, 128:136].rearrange("p (t h) -> p t h", t=T)
        QSLICE = (slice(0, P), slice(P, KEYS))

        def group_heads(g):
            return [(p, i, 2 * g + i) for p in range(2) for i in range(2)]

        def pe_attn(pe):
            w0, w1 = slab(pe, ("w_in_v0", 0)), None
            for t in range(T):
                product_tm(pe, ("va0", t), next_bank(), w0, 512, 0, 512, h_cm, KD, t)
            released(("w_in_v0", 0), ("va0", 1))
            w1 = slab(pe, ("w_in_v1", 0))
            for t in range(T):
                product_tm(pe, ("va1", t), next_bank(), w1, 256, 0, 256, h_cm, KD, t)
            released(("w_in_v1", 0), ("va1", 1))
            for s in range(3):
                w = slab(pe, ("w_in_qk", s))
                for j in range(2):
                    product_cm(pe, ("qk", 4 * s + 2 * j), next_bank(), w, 512,
                               [(2 * j * P, P), ((2 * j + 1) * P, P)], h_cm, KD)
                released(("w_in_qk", s), ("qk", 4 * s + 2))
            pe.wait_ge(named("qk_squared"), 6)
            for b in range(6):
                ps = fill(pe, ("qks", b), next_bank())
                filled(pe.matmul(ps[:, :], headones, SQ[:, 2 * b:2 * b + 2, :], start=True, stop=True), ("qks", b))
            pe.wait_ge(named("qk_ready"), 1)
            for g in range(3):
                for t in range(T):
                    n = P * (t + 1)
                    for p in range(2):
                        key = ("as", g, t, p)
                        ps = fill(pe, key, next_bank())
                        for i in range(2):
                            q = QK[64 * p:64 * p + 64, 2 * g + i, t * P:(t + 1) * P]
                            k = QK[64 * p:64 * p + 64, ATILES + 2 * g + i, 0:n]
                            ins = pe.matmul(ps[:, i * n:(i + 1) * n], q, k, start=True, stop=True)
                        filled(ins, key)
            pe.wait_ge(named("probs_ready"), 1)
            for b in range(9):
                ps = fill(pe, ("pt", b), next_bank())
                for j in range(4):
                    h, blk = divmod(4 * b + j, 3)
                    ins = pe.transpose(ps[:, j * P:(j + 1) * P], PB[:, h, blk * P:(blk + 1) * P], ident)
                filled(ins, ("pt", b))
            for t in range(T):
                drained(pe, ("va0", t))
                drained(pe, ("va1", t))
            for g in range(3):
                for b in range(3 * g, 3 * g + 3):
                    drained(pe, ("pt", b))
                ps = fill(pe, ("ao", g), next_bank())
                for p, i, tile in group_heads(g):
                    h = 4 * g + 2 * p + i
                    c0 = tile * P + 64 * p
                    o = ps[64 * p:64 * p + 64, i * S:(i + 1) * S]
                    pe.matmul(o, VA[:, 0, c0:c0 + HD], PT[:, h, 0:2, :], start=True, stop=False)
                    ins = pe.matmul(o[:, P:S], VA[:, 1, c0:c0 + HD], PT[:, h, 2, :], start=False, stop=True)
                filled(ins, ("ao", g))

        def act_attn(act, ch):
            act.wait_ge(named("y_a_ready"), 1)
            for t in range(T):
                ps = full(act, ("va0", t))
                free(act.copy(VA[:, t, 0:512], ps[:, :]), ("va0", t))
            for t in range(T):
                ps = full(act, ("va1", t))
                free(act.copy(VA[:, t, 512:768], ps[:, 0:256]), ("va1", t))
            for b in range(6):
                ps = full(act, ("qk", 2 * b))
                act.activation(SQ[:, 2 * b:2 * b + 2, :], ps[:, :].rearrange("p (k s) -> p k s", s=S), ACT.Square
                               ).then_inc(named("qk_squared"), 1)
                free(act.copy(QK[:, 2 * b:2 * b + 2, :], ps[:, :].rearrange("p (k s) -> p k s", s=S)), ("qk", 2 * b))
            act.wait_ge(named("qk_meansq"), 1)
            act.activation(SQ, SQ, ACT.Sqrt).then_inc(named("qk_rms"), 1)
            for g in range(3):
                for t in range(T):
                    act.wait_ge(named("row_max_ready"), 2 * g + t + 1)
                    for h in range(4 * g, 4 * g + 4):
                        seg = PB[:, h, QSLICE[t]]
                        ins = act.activation(seg, seg, ACT.Exp, bias=neg_max[:, t, h:h + 1],
                                             accum_out=row_sum[:, t, h:h + 1])
            ins.then_inc(named("row_sum_ready"), 1)
            act.wait_ge(named("row_sum_ready"), 1)
            act.activation(row_lse, row_sum, ACT.Ln).then_inc(named("log_ready"), 1)
            act.wait_ge(named("lse_shifted"), 1)
            act.activation(row_w, row_lse, ACT.Exp).then_inc(named("alpha_exp"), 1)
            for b in range(0, 9, 2):
                ps = full(act, ("pt", b))
                free(act.copy(PT.rearrange("p h b s -> p (h b s)")[:, b * 512:(b + 1) * 512], ps[:, :]), ("pt", b))
            for g in range(3):
                ps = full(act, ("ao", g))
                free(act.copy(YB[:, 2 * g:2 * g + 2, :], ps[:, :].rearrange("p (k s) -> p k s", s=S)), ("ao", g))

        def dve_attn(dve, ch):
            for b in range(6):
                ps = full(dve, ("qks", b))
                ins = nc.vector.tensor_scalar(SQ[:, 2 * b:2 * b + 2, :], ps[:, :].rearrange("p (k s) -> p k s", s=S),
                                              1.0 / HD, RMS_EPS, ALU.mult, ALU.add)
                free(ins, ("qks", b))
            for b in range(6):
                drained(dve, ("qks", b))
                drained(dve, ("qk", 2 * b))
            dve.sem_inc(named("qk_meansq"), 1)
            dve.wait_ge(named("qk_rms"), 1)
            ch.step(nc.vector.reciprocal(SQ, SQ))
            ch.add(nc.vector.tensor_scalar(QK[:, 0:6, :], QK[:, 0:6, :], col("q_norm"), HD ** -0.5, ALU.mult, ALU.mult))
            ch.add(nc.vector.tensor_scalar(QK[:, 6:12, :], QK[:, 6:12, :], col("k_norm"), None, ALU.mult))
            ch.fence()
            nc.vector.tensor_tensor(QK, QK, SQ, ALU.mult).then_inc(named("qk_ready"), 1)
            dve.wait_ge(named("qk_ready"), 1)
            dve.wait_ge(named("masks_loaded"), 16)
            for g in range(3):
                for t in range(T):
                    n = P * (t + 1)
                    mask = const(f"mask{g}", KEYS)[:, QSLICE[t]]
                    for p in range(2):
                        ps = full(dve, ("as", g, t, p))
                        h = 4 * g + 2 * p
                        free(nc.vector.tensor_tensor(PB[:, h:h + 2, QSLICE[t]],
                                                     ps[:, 0:2 * n].rearrange("p (i s) -> p i s", i=2),
                                                     times(mask, 2), ALU.add), ("as", g, t, p))
                        drained(dve, ("as", g, t, p))
                    ch.step(nc.vector.tensor_reduce(row_max[:, t, 4 * g:4 * g + 4], PB[:, 4 * g:4 * g + 4, QSLICE[t]],
                                                    AX, ALU.max))
                    nc.vector.tensor_scalar(neg_max[:, t, 4 * g:4 * g + 4], row_max[:, t, 4 * g:4 * g + 4], -1.0, None,
                                            ALU.mult).then_inc(named("row_max_ready"), 1)
            dve.wait_ge(named("log_ready"), 1)
            ch.step(nc.vector.tensor_tensor(row_lse, row_lse, row_max, ALU.add))
            ch.step(nc.vector.tensor_tensor(lse_max, row_lse[:, :, 0:4], row_lse[:, :, 4:8], ALU.max))
            ch.step(nc.vector.tensor_tensor(lse_max, lse_max, row_lse[:, :, 8:12], ALU.max))
            for g in range(3):
                l = row_lse[:, :, 4 * g:4 * g + 4]
                ins = nc.vector.tensor_tensor(l, l, lse_max, ALU.subtract)
                ch.add(ins)
            ch.fence()
            dve.sem_inc(named("lse_shifted"), 1)
            dve.wait_ge(named("alpha_exp"), 1)
            ch.step(nc.vector.tensor_tensor(w_sum, row_w[:, :, 0:4], row_w[:, :, 4:8], ALU.add))
            ch.step(nc.vector.tensor_tensor(w_sum, w_sum, row_w[:, :, 8:12], ALU.add))
            for g in range(3):
                s_ = row_sum[:, :, 4 * g:4 * g + 4]
                ch.add(nc.vector.tensor_tensor(s_, s_, w_sum, ALU.mult))
            ch.fence()
            ch.step(nc.vector.reciprocal(row_sum, row_sum))
            ch.step(nc.vector.tensor_tensor(row_w, row_w, row_sum, ALU.mult))
            for t in range(T):
                seg = PB[:, :, QSLICE[t]]
                ch.add(nc.vector.tensor_tensor(seg, seg, spread(row_w[:, t, :], P * (t + 1)), ALU.mult))
            ch.fence()
            dve.sem_inc(named("probs_ready"), 1)
            for b in range(1, 9, 2):
                ps = full(dve, ("pt", b))
                free(nc.vector.tensor_copy(PT.rearrange("p h b s -> p (h b s)")[:, b * 512:(b + 1) * 512], ps[:, :]),
                     ("pt", b))

        def pe_merge1(pe):
            for s in range(2):
                w = slab(pe, ("w_proj_rwkv", s))
                for j in range(2):
                    product_cm(pe, ("pr", 4 * s + 2 * j), next_bank(), w, 512,
                               [(2 * j * P, P), ((2 * j + 1) * P, P)], Y_A, KD)
                released(("w_proj_rwkv", s), ("pr", 4 * s + 2))
            for g in range(3):
                drained(pe, ("ao", g))
            for s in range(2):
                w = slab(pe, ("w_proj_attn", s))
                for j in range(2):
                    product_cm(pe, ("pa", 4 * s + 2 * j), next_bank(), w, 512,
                               [(2 * j * P, P), ((2 * j + 1) * P, P)], YB, ATILES)
                released(("w_proj_attn", s), ("pa", 4 * s + 2))
            pe.wait_ge(named("merged"), 1)
            pe_out(pe, "w_out", MERGED)

        def pe_out(pe, name, src):
            for s in range(2):
                w = slab(pe, (name, s))
                for t in range(T):
                    product_tm(pe, (name, s, t), next_bank(), w, 512, 0, 512, src, KD, t)
                released((name, s), (name, s, 1))

        def dve_merge(dve, ch, first, second, gates, n, dst, tmp):
            for branch, out_, g0 in ((first, dst, 0), (second, tmp, 8)):
                for b in range(0, 8, 2):
                    ps = full(dve, (*branch, b))
                    free(nc.vector.tensor_tensor(out_[:, b:b + 2, :], ps[:, :].rearrange("p (k s) -> p k s", s=S),
                                                 gates[:, g0 + b:g0 + b + 2, :], ALU.mult), (*branch, b))
            for b in range(0, 8, 2):
                drained(dve, (*first, b))
                drained(dve, (*second, b))
            nc.vector.tensor_tensor(dst, dst, tmp, ALU.add).then_inc(named("merged"), 1)

        def dve_merge1(dve, ch):
            for g in range(3):
                drained(dve, ("ao", g))
            for tile in range(0, 16, 2):
                drained(dve, ("gate", tile))
            dve_merge(dve, ch, ("pr",), ("pa",), gates, 1, MERGED, MTMP)
            for s in range(2):
                for t in range(T):
                    ps = full(dve, ("w_out", s, t))
                    part = x_tm[:, t, s * 512:(s + 1) * 512]
                    free(nc.vector.tensor_tensor(part, part, ps[:, :], ALU.add), ("w_out", s, t))

        def x_after_out(eng):
            for s in range(2):
                for t in range(T):
                    drained(eng, ("w_out", s, t))

        def piece(at, k, s=S):
            return arena[:, at:at + k * s].rearrange("p (k s) -> p k s", s=s)

        QD, KDF = piece(0, 8), piece(2048, 8)
        VD = arena[:, 4096:6144].rearrange("p (t d) -> p t d", t=T)
        gates2 = piece(6144, 16)
        OA = piece(10240, 8)
        Q96, K96 = piece(12288, 8), piece(14336, 8)
        VM = arena[:, 16384:17408].rearrange("p (t d) -> p t d", t=T)
        OB = piece(17408, 4)
        LAT, LSQ = piece(18432, 5), piece(19712, 5)
        P2 = arena[:, 18432:19968].rearrange("p (h s) -> p h s", s=KEYS)
        PT2 = arena[:, 19968:21504].rearrange("p (h b s) -> p h b s", b=3, s=P)
        WD = arena[:, 21504:22272].rearrange("p (h s) -> p h s", s=KEYS)
        COS, SIN = arena[:, 22272:22528], arena[:, 22528:22784]
        ROPE = [arena[:, 22784 + 256 * i:22784 + 256 * (i + 1)] for i in range(3)]
        BIAS = arena[:, 23552:23552 + DHEADS * KEYS].rearrange("p (h s) -> p h s", s=KEYS)
        POSK, POSQ = arena[:, 0:256], arena[:, 256:258]
        DIST = arena[:, 258:642]
        REACHED = [arena[:, 642 + i * KEYS:642 + (i + 1) * KEYS] for i in range(STEPS)]
        TAB, DELTA = arena[:, 3400:3656], arena[:, 3656:3656 + 8 * (STEPS * U_DENSE + 1)]
        STEP_NOW, THR_NOW = arena[:, 3968:3968 + 8 * STEPS], arena[:, 4000:4000 + STEPS]
        ANG, KR = arena[:, 2048:2304], arena[:, 2304:2560]
        LAMV = arena[:, 2560:3072].rearrange("p (l f d) -> p l f d", l=2, f=4)
        POSI = arena[:, 3072:3330].bitcast(I32)
        neg_lam = stat[:, 16:18]
        E_TM, M2, M2T = tm(0), cm(8), cm(0)
        PLE_CM = arena[:, 4096:4608].rearrange("p (k s) -> p k s", s=S)
        PLE_TM = arena[:, 4608:5120].rearrange("p (t d) -> p t d", t=T)
        ROUTER = arena[:, 5120:5184]
        LOGITS = arena[:, 5184:5200].rearrange("p (t e) -> p t e", t=T)
        RT = [arena[:, 5200 + 16 * i:5216 + 16 * i].rearrange("p (t e) -> p t e", t=T) for i in range(6)]
        COMB = arena[:, 5328:5344].rearrange("p (t e) -> p t e", t=T)
        RC = [arena[:, 5344 + 2 * i:5346 + 2 * i] for i in range(8)]
        PLACE = arena[:, 5376:5392].rearrange("p (t e) -> p t e", t=T)
        QUEUED = arena[:, 5392:5400]
        LONGEST = arena[:, 5400:5401]
        OVER = arena[:, 5402:5402 + MAX_PASSES - 1]
        PASSES = arena[:, 5401:5402].bitcast(I32)
        QUEUE = arena[:, 6144:6144 + N_EXPERTS * D].rearrange("p (e d) -> p e d", e=N_EXPERTS)[
            :, :, 0:KD * PLACES].rearrange("p e (k s) -> p e k s", s=PLACES)
        SUMS = arena[0:PLACES, 6144:6144 + N_EXPERTS * D].rearrange("p (e d) -> p e d", e=N_EXPERTS)
        PICK = arena[:, 14336:14336 + T * N_EXPERTS * PLACES].rearrange("p (t e s) -> p t e s", t=T, e=N_EXPERTS)
        WEIGHT = arena[:, 16384:16384 + T * N_EXPERTS * PLACES].rearrange("p (t e s) -> p t e s", t=T, e=N_EXPERTS)
        RETURN = arena[0:PLACES, 18432:20480].rearrange("p (e s) -> p e s", e=N_EXPERTS)
        rmax2 = ff[:, 0, 0:32].rearrange("p (t h) -> p t h", t=T)
        nmax2 = ff[:, 0, 32:64].rearrange("p (t h) -> p t h", t=T)
        rsum2 = ff[:, 0, 64:96].rearrange("p (t h) -> p t h", t=T)
        lnrow = xn
        bnst = ff[:, 1, 0:24].rearrange("p (t n) -> p t n", t=T)
        bnag = ff[:, 1, 32:36].rearrange("p (t n) -> p t n", t=T)
        lstd = ff[:, 1, 40:42]

        TWO_PI = 2.0 * math.pi
        C1 = 6.28125
        C2 = float(np.float32(TWO_PI - C1))
        C3 = float(np.float32(TWO_PI - C1 - C2))
        ROUND = 12582912.0

        def dve_tables(dve, ch):
            x_after_out(dve)
            dve.wait_ge(named("tables_loaded"), 16 * 5)
            v = nc.vector
            ch.add(v.tensor_copy(POSK, POSI[:, 0:256]))
            ch.add(v.tensor_copy(POSQ, POSI[:, 256:258]))
            ch.fence()
            for t, (lo, n) in enumerate(((0, P), (P, S))):
                ch.add(v.tensor_scalar(DIST[:, lo:lo + n], POSK[:, 0:n], POSQ[:, t:t + 1], -1.0, ALU.subtract, ALU.mult))
            ch.add(v.tensor_tensor(DELTA[:, 0:248], TAB[:, 8:256], TAB[:, 0:248], ALU.subtract))
            ch.add(v.memset(DELTA[:, 248:], 0.0))
            for h in range(DHEADS):
                ch.add(v.tensor_scalar(BIAS[:, h, :], const("causal", KEYS), TAB[:, h:h + 1], None, ALU.add))
            ch.fence()
            rows = slice(64, 96)
            ang, kr = ANG[rows, :], KR[rows, :]
            ch.step(v.tensor_scalar(ang, POSK[rows, :], const("freq", 2)[rows, 0:1], None, ALU.mult))
            ch.step(v.tensor_scalar(kr, ang, 1.0 / TWO_PI, ROUND, ALU.mult, ALU.add))
            ch.step(v.tensor_scalar(kr, kr, -ROUND, None, ALU.add))
            for c in (C1, C2, C3):
                ch.step(v.scalar_tensor_tensor(ang, kr, -c, ang, ALU.mult, ALU.add))
            ch.step(v.tensor_scalar(kr, ang, math.pi / 2, -TWO_PI, ALU.is_gt, ALU.mult))
            ch.step(v.scalar_tensor_tensor(kr, ang, math.pi / 2, kr, ALU.add, ALU.add))
            ch.step(v.tensor_scalar(kr, kr, math.pi, -math.pi, ALU.min, ALU.max))
            ch.step(v.tensor_scalar(ang, ang, math.pi, -math.pi, ALU.min, ALU.max))
            dve.sem_inc(named("angles_ready"), 1)
            for l in range(DEPTH_2):
                for f in range(2):
                    ch.step(v.tensor_tensor(LAMV[:, l, 2 * f, :], LAMV[:, l, 2 * f, :], LAMV[:, l, 2 * f + 1, :], ALU.mult))
                    ch.step(v.tensor_reduce(stat[:, 20 + 2 * l + f:21 + 2 * l + f], LAMV[:, l, 2 * f, :], AX, ALU.add))
            dve.sem_inc(named("lambda_dots"), 1)
            dve.wait_ge(named("tables_act"), 3)
            ch.step(v.tensor_scalar(SIN[rows, :], SIN[rows, :], const("freq", 2)[rows, 1:2], None, ALU.mult))
            for l in range(DEPTH_2):
                init = 0.8 - 0.6 * math.exp(-0.3 * l)
                ch.step(v.tensor_tensor(neg_lam[:, l:l + 1], stat[:, 25 + 2 * l:26 + 2 * l], stat[:, 24 + 2 * l:25 + 2 * l], ALU.subtract))
                ch.step(v.tensor_scalar(neg_lam[:, l:l + 1], neg_lam[:, l:l + 1], -init, None, ALU.add))

        def act_tables(act, ch):
            act.wait_ge(named("angles_ready"), 1)
            act.activation(SIN[64:96, :], ANG[64:96, :], ACT.Sin).then_inc(named("tables_act"), 1)
            act.activation(COS[64:96, :], KR[64:96, :], ACT.Sin).then_inc(named("tables_act"), 1)
            act.wait_ge(named("lambda_dots"), 1)
            act.activation(stat[:, 24:28], stat[:, 20:24], ACT.Exp).then_inc(named("tables_act"), 1)

        def dve_bias(u):
            v = nc.vector
            done, n = named("bias_steps"), u * (2 + STEPS + STEPS * DHEADS)
            v.tensor_copy(STEP_NOW, DELTA[:, bass.ds(u * (8 * STEPS), 8 * STEPS)]).then_inc(done, 1)
            v.tensor_copy(THR_NOW, const("thresholds", STEPS * U_DENSE)[:, bass.ds(u * STEPS, STEPS)]).then_inc(done, 1)
            v.wait_ge(done, n + 2)
            for r in range(STEPS):
                v.tensor_scalar(REACHED[r], DIST, THR_NOW[:, r:r + 1], None, ALU.is_ge).then_inc(done, 1)
            for r in range(STEPS):
                v.wait_ge(done, n + 2 + STEPS + r * DHEADS)
                for h in range(DHEADS):
                    v.scalar_tensor_tensor(BIAS[:, h, :], REACHED[r], STEP_NOW[:, r * 8 + h:r * 8 + h + 1], BIAS[:, h, :],
                                           ALU.mult, ALU.add).then_inc(done, 1)
            v.wait_ge(done, n + 2 + STEPS + STEPS * DHEADS)

        def dve_layernorm(dve, ch, m):
            v = nc.vector
            for t in range(T):
                for half in range(2):
                    ch.add(v.bn_stats(bnst[:, t, 6 * half:6 * half + 6], x_tm[:, t, half * 512:half * 512 + 512]))
            ch.fence()
            for t in range(T):
                ch.add(v.bn_aggr(bnag[:, t, :], bnst[:, t, :]))
            ch.fence()
            v.tensor_scalar(lstd, bnag[:, :, 1], EPS, None, ALU.add).then_inc(named("ln_var"), 1)
            dve.wait_ge(named("ln_std"), m + 1)
            ch.step(v.reciprocal(lstd, lstd))
            dve.wait_ge(named("ln_rows"), 16 * 2 * (m + 1))
            for t in range(T):
                ch.add(v.tensor_scalar(x_tm[:, t, :], x_tm[:, t, :], bnag[:, t, 0:1], lstd[:, t:t + 1],
                                       ALU.subtract, ALU.mult))
            ch.fence()
            ch.step(v.tensor_tensor(x_tm[:, :, :], x_tm[:, :, :], times(lnrow[:, 0, :], T), ALU.mult))
            v.tensor_tensor(x_tm[:, :, :], x_tm[:, :, :], times(lnrow[:, 1, :], T), ALU.add).then_inc(named("x_normed"), 1)
            dve.wait_ge(named("x_normed"), m + 1)

        def act_layernorm(act, m):
            act.wait_ge(named("ln_var"), m + 1)
            act.activation(lstd, lstd, ACT.Sqrt).then_inc(named("ln_std"), 1)

        def pool_layernorm(pool, m):
            if m:
                pool.wait_ge(named("x_normed"), m)
            else:
                h_written(pool, ("norm", "ffn2"))
            for j, name in enumerate(("ln_gain", "ln_bias")):
                pool.dma_start(lnrow[:, j, :], dram[name][m:m + 1, :].broadcast_to([P, D])
                               ).then_inc(named("ln_rows"), 16)

        def pool_extras(pool, l):
            pool.wait_ge(named("x_normed"), 2 * l + 1)
            pool.dma_start(PLE_TM, dram["ple"][l]).then_inc(named("ple_loaded"), 16)
            if l == 1:
                pool.dma_start(ROUTER, dram["router"]).then_inc(named("router_loaded"), 16)

        def pe_mixer2(pe, l):
            if l == 0:
                x_after("ffn2")(pe)
            else:
                pe.wait_ge(named("x_normed"), 2 * l)
            pe_turn(pe, ("turn", 2 * l), x_tm)
            h_written(pe, ("turn", 2 * l))
            w = slab(pe, (f"lat_{l}", 0))
            product_cm(pe, ("lat", l, 0), next_bank(), w, 512, [(0, P), (P, P)], h_cm, KD)
            product_cm(pe, ("lat", l, 2), next_bank(), w, 512, [(2 * P, P), (3 * P, P)], h_cm, KD)
            released((f"lat_{l}", 0), ("lat", l, 2))
            w = slab(pe, (f"latr_{l}", 0))
            product_cm(pe, ("lat", l, 4), next_bank(), w, 192, [(0, P)], h_cm, KD)
            ps = fill(pe, ("kr", l), next_bank())
            for j in range(2):
                for k in range(KD):
                    ins = pe.matmul(ps[64:96, j * S:(j + 1) * S], w[:, k * 192 + 128 + 32 * j:k * 192 + 160 + 32 * j],
                                    h_cm[:, k, :], start=k == 0, stop=k == KD - 1)
            filled(ins, ("kr", l))
            released((f"latr_{l}", 0), ("kr", l))
            for s in range(2):
                w = slab(pe, (f"dv_{l}", s))
                for t in range(T):
                    product_tm(pe, ("dv", l, s, t), next_bank(), w, 512, 0, 512, h_cm, KD, t)
                released((f"dv_{l}", s), ("dv", l, s, 1))
            pe.wait_ge(named("lat_squared"), 3 * (l + 1))
            ps = fill(pe, ("ls", l), next_bank())
            for j, ks in enumerate((range(0, NQ), range(NQ, NQ + NKV))):
                for k in ks:
                    ins = pe.matmul(ps[:, j * S:(j + 1) * S], ones, LSQ[:, k, :], start=k == ks[0], stop=k == ks[-1])
            filled(ins, ("ls", l))
            for name, key, count in (("dqk_", "dqk", 4), ("g2_", "g2", 4)):
                for s in range(count):
                    w = slab(pe, (f"{name}{l}", s))
                    for j in range(2):
                        product_cm(pe, (key, l, 4 * s + 2 * j), next_bank(), w, 512,
                                   [(2 * j * P, P), ((2 * j + 1) * P, P)], h_cm, KD)
                    released((f"{name}{l}", s), (key, l, 4 * s + 2))
            pe.wait_ge(named("lat_ready"), l + 1)
            w = slab(pe, (f"uq_{l}", 0))
            for hp in range(4):
                product_cm(pe, ("uq", l, hp), next_bank(), w, 1024, [(2 * hp * 96, 96), ((2 * hp + 1) * 96, 96)], LAT, NQ)
                ps = fill(pe, ("ur", l, hp), next_bank())
                for j in range(2):
                    c0 = 768 + (2 * hp + j) * 32
                    for k in range(NQ):
                        ins = pe.matmul(ps[64:96, j * S:(j + 1) * S], w[:, k * 1024 + c0:k * 1024 + c0 + 32], LAT[:, k, :],
                                        start=k == 0, stop=k == NQ - 1)
                filled(ins, ("ur", l, hp))
            released((f"uq_{l}", 0), ("ur", l, 3))
            w = slab(pe, (f"ukv_{l}", 0))
            for hp in range(4):
                product_cm(pe, ("uk", l, hp), next_bank(), w, 1024, [(2 * hp * 64, 64), ((2 * hp + 1) * 64, 64)],
                           LAT[:, NQ:, :], NKV)
            for t in range(T):
                product_tm(pe, ("uv", l, t), next_bank(), w, 1024, 512, 512, LAT[:, NQ:, :], NKV, t)
            released((f"ukv_{l}", 0), ("uv", l, 1))
            for tile in range(0, 16, 2):
                drained(pe, ("dqk", l, tile))
            for a in range(4):
                for t in range(T):
                    n = P * (t + 1)
                    for m in range(2):
                        key = ("ds", l, a, t, m)
                        ps = fill(pe, key, next_bank())
                        for j in range(2):
                            ins = pe.matmul(ps[:, j * n:(j + 1) * n], QD[64 * m:64 * m + 64, 2 * a + j, t * P:(t + 1) * P],
                                            KDF[64 * m:64 * m + 64, 2 * a + j, 0:n], start=True, stop=True)
                        filled(ins, key)
                pe.wait_ge(named("diff_weights"), 4 * l + a + 1)
                for b, blocks in enumerate((range(0, 4), range(4, 6))):
                    ps = fill(pe, ("dt", l, a, b), next_bank())
                    for i, f in enumerate(blocks):
                        ins = pe.transpose(ps[:, i * P:(i + 1) * P], WD[:, f // 3, (f % 3) * P:(f % 3 + 1) * P], ident)
                    filled(ins, ("dt", l, a, b))
                for b in range(2):
                    drained(pe, ("dt", l, a, b))
                if a == 0:
                    for s in range(2):
                        for t in range(T):
                            drained(pe, ("dv", l, s, t))
                ps = fill(pe, ("do", l, a), next_bank())
                for j in range(2):
                    c0 = (2 * a + j) * P
                    pe.matmul(ps[:, j * S:(j + 1) * S], VD[:, 0, c0:c0 + P], PT2[:, j, 0:2, :], start=True, stop=False)
                    ins = pe.matmul(ps[:, j * S + P:(j + 1) * S], VD[:, 1, c0:c0 + P], PT2[:, j, 2, :], start=False, stop=True)
                filled(ins, ("do", l, a))
            pe.wait_ge(named("mla_qk"), 5 * (l + 1))
            for hp in range(4):
                drained(pe, ("uk", l, hp))
            for g in range(2):
                for t in range(T):
                    n = P * (t + 1)
                    for jp in range(2):
                        key = ("ms", l, g, t, jp)
                        ps = fill(pe, key, next_bank())
                        for j in range(2):
                            h = 4 * g + 2 * jp + j
                            ins = pe.matmul(ps[:, j * n:(j + 1) * n], Q96[0:96, h, t * P:(t + 1) * P], K96[0:96, h, 0:n],
                                            start=True, stop=True)
                        filled(ins, key)
                pe.wait_ge(named("mla_weights"), 2 * l + g + 1)
                for b in range(3):
                    ps = fill(pe, ("mt", l, g, b), next_bank())
                    for i in range(4):
                        h, blk = divmod(4 * b + i, 3)
                        ins = pe.transpose(ps[:, i * P:(i + 1) * P], P2[:, h, blk * P:(blk + 1) * P], ident)
                    filled(ins, ("mt", l, g, b))
                for b in range(3):
                    drained(pe, ("mt", l, g, b))
                if g == 0:
                    for t in range(T):
                        drained(pe, ("uv", l, t))
                ps = fill(pe, ("mo", l, g), next_bank())
                for r in range(4):
                    h, i, p = 4 * g + r, r // 2, r % 2
                    o = ps[64 * p:64 * p + 64, i * S:(i + 1) * S]
                    pe.matmul(o, VM[:, 0, h * HD:(h + 1) * HD], PT2[:, r, 0:2, :], start=True, stop=False)
                    ins = pe.matmul(o[:, P:S], VM[:, 1, h * HD:(h + 1) * HD], PT2[:, r, 2, :], start=False, stop=True)
                filled(ins, ("mo", l, g))
            pe.wait_ge(named("oa_squared"), l + 1)
            for b in range(4):
                ps = fill(pe, ("dn", l, b), next_bank())
                filled(pe.matmul(ps[:, :], ones, QD[:, 2 * b:2 * b + 2, :], start=True, stop=True), ("dn", l, b))
            for g in range(2):
                drained(pe, ("mo", l, g))
            pe.wait_ge(named("oa_ready"), l + 1)
            for s in range(2):
                w = slab(pe, (f"bdiff_{l}", s))
                for j in range(2):
                    product_cm(pe, ("bd", l, 4 * s + 2 * j), next_bank(), w, 512,
                               [(2 * j * P, P), ((2 * j + 1) * P, P)], OA, KD)
                released((f"bdiff_{l}", s), ("bd", l, 4 * s + 2))
            w = slab(pe, (f"bmla_{l}", 0))
            for b in range(0, 8, 2):
                product_cm(pe, ("bm", l, b), next_bank(), w, 1024, [(b * P, P), ((b + 1) * P, P)], OB, 4)
            released((f"bmla_{l}", 0), ("bm", l, 6))
            pe.wait_ge(named("merged"), 2 + l)
            pe_out(pe, f"out2_{l}", KDF)

        def act_softmax(act, l, name, groups, base):
            for t in range(T):
                act.wait_ge(named("max2_ready"), base + t + 1)
                for r in range(4):
                    seg = P2[:, r, QSLICE[t]]
                    act.activation(seg, seg, ACT.Exp, bias=nmax2[:, t, 4 * groups + r:4 * groups + r + 1],
                                   accum_out=rsum2[:, t, 4 * groups + r:4 * groups + r + 1]
                                   ).then_inc(named("exp2"), 1)

        def act_mixer2(act, ch, l):
            act_turned(act, ("turn", 2 * l), None)
            for b in (0, 2, 4):
                ps = full(act, ("lat", l, b))
                k = 2 if b < 4 else 1
                src = ps[:, 0:k * S].rearrange("p (k s) -> p k s", s=S)
                act.activation(LSQ[:, b:b + k, :], src, ACT.Square).then_inc(named("lat_squared"), 1)
                free(act.copy(LAT[:, b:b + k, :], src), ("lat", l, b))
            for s in range(2):
                for t in range(T):
                    ps = full(act, ("dv", l, s, t))
                    free(act.copy(VD[:, t, s * 512:(s + 1) * 512], ps[:, :]), ("dv", l, s, t))
            act.wait_ge(named("lat_meansq"), l + 1)
            act.activation(ff[:, 2, :], ff[:, 2, :], ACT.Sqrt).then_inc(named("lat_rms"), 1)
            for tile in range(0, 16, 2):
                ps = full(act, ("dqk", l, tile))
                dst = (QD, KDF)[tile // 8][:, tile % 8:tile % 8 + 2, :]
                free(act.copy(dst, ps[:, :].rearrange("p (k s) -> p k s", s=S)), ("dqk", l, tile))
            for tile in range(0, 16, 2):
                ps = full(act, ("g2", l, tile))
                for j in range(2):
                    ins = act.activation(gates2[:, tile + j, :], ps[:, j * S:(j + 1) * S], ACT.Sigmoid,
                                         bias=col(f"b_gate{l}", tile + j))
                free(ins, ("g2", l, tile))
            for hp in range(4):
                ps = full(act, ("uq", l, hp))
                free(act.copy(Q96[0:96, 2 * hp:2 * hp + 2, :], ps[0:96, :].rearrange("p (k s) -> p k s", s=S)), ("uq", l, hp))
            for hp in range(4):
                ps = full(act, ("uk", l, hp))
                free(act.copy(K96[0:64, 2 * hp:2 * hp + 2, :], ps[0:64, :].rearrange("p (k s) -> p k s", s=S)), ("uk", l, hp))
            for t in range(T):
                ps = full(act, ("uv", l, t))
                free(act.copy(VM[:, t, :], ps[:, :]), ("uv", l, t))
            for a in range(4):
                act_softmax(act, l, "diff", a, 12 * l + 2 * a)
                ps = full(act, ("dt", l, a, 0))
                free(act.copy(PT2.rearrange("p h b s -> p (h b s)")[:, 0:512], ps[:, :]), ("dt", l, a, 0))
                ps = full(act, ("do", l, a))
                free(act.copy(OA[:, 2 * a:2 * a + 2, :], ps[:, :].rearrange("p (k s) -> p k s", s=S)), ("do", l, a))
            for a in range(4):
                drained(act, ("do", l, a))
            act.activation(QD, OA, ACT.Square).then_inc(named("oa_squared"), 1)
            for g in range(2):
                act_softmax(act, l, "mla", g, 12 * l + 8 + 2 * g)
                for b in (0, 2):
                    ps = full(act, ("mt", l, g, b))
                    free(act.copy(PT2.rearrange("p h b s -> p (h b s)")[:, b * 512:(b + 1) * 512], ps[:, :]), ("mt", l, g, b))
                ps = full(act, ("mo", l, g))
                free(act.copy(OB[:, 2 * g:2 * g + 2, :], ps[:, :].rearrange("p (k s) -> p k s", s=S)), ("mo", l, g))
            act.wait_ge(named("oa_meansq"), l + 1)
            act.activation(QD, QD, ACT.Sqrt).then_inc(named("oa_rms"), 1)

        def dve_row_max(dve, ch, t, g):
            v = nc.vector
            ch.step(v.tensor_reduce(rmax2[:, t, 4 * g:4 * g + 4], P2[:, 0:4, QSLICE[t]], AX, ALU.max))
            v.tensor_scalar(nmax2[:, t, 4 * g:4 * g + 4], rmax2[:, t, 4 * g:4 * g + 4], -1.0, None, ALU.mult
                            ).then_inc(named("max2_ready"), 1)

        def dve_mixer2(dve, ch, l):
            v = nc.vector
            dve_turned(dve, ("turn", 2 * l), None)
            rows = slice(64, 96)
            ps = full(dve, ("kr", l))
            ch.add(v.tensor_tensor(ROPE[0][rows, :], ps[rows, 0:S], COS[rows, :], ALU.mult))
            free(v.tensor_tensor(ROPE[1][rows, :], ps[rows, S:2 * S], SIN[rows, :], ALU.mult), ("kr", l))
            drained(dve, ("kr", l))
            ch.step(v.tensor_tensor(ROPE[2][rows, :], ROPE[0][rows, :], ROPE[1][rows, :], ALU.add))
            v.tensor_copy(K96[rows, :, :], times(ROPE[2][rows, :], MHEADS)).then_inc(named("mla_qk"), 1)
            ps = full(dve, ("ls", l))
            ch.add(v.tensor_scalar(ff[:, 2, 0:S], ps[:, 0:S], 1.0 / (NQ * P), EPS, ALU.mult, ALU.add))
            free(v.tensor_scalar(ff[:, 2, S:2 * S], ps[:, S:2 * S], 1.0 / (NKV * P), EPS, ALU.mult, ALU.add), ("ls", l))
            drained(dve, ("ls", l))
            dve.sem_inc(named("lat_meansq"), 1)
            dve.wait_ge(named("lat_rms"), l + 1)
            ch.step(v.reciprocal(ff[:, 2, :], ff[:, 2, :]))
            for b in (0, 2, 4):
                drained(dve, ("lat", l, b))
            for k in range(NQ + NKV):
                j = int(k >= NQ)
                gain = col(f"mlakv{l}", k - NQ) if j else col(f"mlaq{l}", k)
                ch.add(v.scalar_tensor_tensor(LAT[:, k, :], LAT[:, k, :], gain, ff[:, 2, j * S:(j + 1) * S], ALU.mult, ALU.mult))
            ch.fence()
            dve.sem_inc(named("lat_ready"), 1)
            for hp in range(4):
                drained(dve, ("uq", l, hp))
                ps = full(dve, ("ur", l, hp))
                q = Q96[rows, 2 * hp:2 * hp + 2, :]
                t0 = ff[rows, 2, :].rearrange("p (k s) -> p k s", s=S)
                t1 = ff[rows, 3, :].rearrange("p (k s) -> p k s", s=S)
                ch.add(v.tensor_tensor(t0, q, times(COS[rows, :], 2), ALU.mult))
                free(v.tensor_tensor(t1, ps[rows, :].rearrange("p (k s) -> p k s", s=S), times(SIN[rows, :], 2), ALU.mult),
                     ("ur", l, hp))
                ch.fence()
                drained(dve, ("ur", l, hp))
                v.tensor_tensor(q, t0, t1, ALU.add).then_inc(named("mla_qk"), 1)
                dve.wait_ge(named("mla_qk"), 5 * l + hp + 2)
            full(dve, ("uv", l, 1))
            for a in range(4):
                if a:
                    full(dve, ("dt", l, a - 1, 1))
                for t in range(T):
                    n = P * (t + 1)
                    for m in range(2):
                        ps = full(dve, ("ds", l, a, t, m))
                        free(v.scalar_tensor_tensor(P2[:, m:4:2, QSLICE[t]], ps[:, 0:2 * n].rearrange("p (j s) -> p j s", j=2),
                                                    HD ** -0.5, BIAS[:, 2 * a:2 * a + 2, QSLICE[t]], ALU.mult, ALU.add),
                             ("ds", l, a, t, m))
                        drained(dve, ("ds", l, a, t, m))
                    dve_row_max(dve, ch, t, a)
                dve.wait_ge(named("exp2"), 24 * 2 * l + 8 * a + 8)
                ch.step(v.reciprocal(rsum2[:, :, 4 * a:4 * a + 4], rsum2[:, :, 4 * a:4 * a + 4]))
                for j in range(2):
                    r = rsum2[:, :, 4 * a + 2 * j + 1]
                    ch.add(v.tensor_scalar(r, r, neg_lam[:, l:l + 1], None, ALU.mult))
                ch.fence()
                for t in range(T):
                    for j in range(2):
                        r = 4 * a + 2 * j
                        ch.add(v.tensor_scalar(WD[:, j, QSLICE[t]], P2[:, 2 * j, QSLICE[t]], rsum2[:, t, r:r + 1], None, ALU.mult))
                ch.fence()
                for t in range(T):
                    for j in range(2):
                        r = 4 * a + 2 * j + 1
                        ch.add(v.scalar_tensor_tensor(WD[:, j, QSLICE[t]], P2[:, 2 * j + 1, QSLICE[t]], rsum2[:, t, r:r + 1],
                                                      WD[:, j, QSLICE[t]], ALU.mult, ALU.add))
                ch.fence()
                dve.sem_inc(named("diff_weights"), 1)
                ps = full(dve, ("dt", l, a, 1))
                free(v.tensor_copy(PT2.rearrange("p h b s -> p (h b s)")[:, 512:768], ps[:, 0:256]), ("dt", l, a, 1))
            for g in range(2):
                if g:
                    full(dve, ("mt", l, g - 1, 2))
                for t in range(T):
                    n = P * (t + 1)
                    causal = const("causal", KEYS)[:, QSLICE[t]]
                    for jp in range(2):
                        ps = full(dve, ("ms", l, g, t, jp))
                        free(v.scalar_tensor_tensor(P2[:, 2 * jp:2 * jp + 2, QSLICE[t]],
                                                    ps[:, 0:2 * n].rearrange("p (j s) -> p j s", j=2),
                                                    MLA_SCALE, times(causal, 2), ALU.mult, ALU.add), ("ms", l, g, t, jp))
                        drained(dve, ("ms", l, g, t, jp))
                    dve_row_max(dve, ch, t, g)
                dve.wait_ge(named("exp2"), 24 * 2 * l + 32 + 8 * g + 8)
                ch.step(v.reciprocal(rsum2[:, :, 4 * g:4 * g + 4], rsum2[:, :, 4 * g:4 * g + 4]))
                for t in range(T):
                    seg = P2[:, :, QSLICE[t]]
                    ch.add(v.tensor_tensor(seg, seg, spread(rsum2[:, t, 4 * g:4 * g + 4], P * (t + 1)), ALU.mult))
                ch.fence()
                dve.sem_inc(named("mla_weights"), 1)
                ps = full(dve, ("mt", l, g, 1))
                free(v.tensor_copy(PT2.rearrange("p h b s -> p (h b s)")[:, 512:1024], ps[:, :]), ("mt", l, g, 1))
            for b in range(4):
                ps = full(dve, ("dn", l, b))
                free(v.tensor_scalar(QD[:, 2 * b:2 * b + 2, :], ps[:, :].rearrange("p (k s) -> p k s", s=S), 1.0 / P, EPS,
                                     ALU.mult, ALU.add), ("dn", l, b))
                drained(dve, ("dn", l, b))
            dve.sem_inc(named("oa_meansq"), 1)
            dve.wait_ge(named("oa_rms"), l + 1)
            ch.step(v.reciprocal(QD, QD))
            init = 0.8 - 0.6 * math.exp(-0.3 * l)
            ch.step(v.tensor_tensor(OA, OA, QD, ALU.mult))
            v.tensor_scalar(OA, OA, col(f"subln{l}"), 1.0 - init, ALU.mult, ALU.mult).then_inc(named("oa_ready"), 1)
            for tile in range(0, 16, 2):
                drained(dve, ("g2", l, tile))
            dve_merge(dve, ch, ("bd", l), ("bm", l), gates2, 2 + l, KDF, QD)
            for s in range(2):
                for t in range(T):
                    ps = full(dve, (f"out2_{l}", s, t))
                    part = x_tm[:, t, s * 512:(s + 1) * 512]
                    free(v.scalar_tensor_tensor(part, part, ALPHA, ps[:, :], ALU.mult, ALU.add), (f"out2_{l}", s, t))
                    drained(dve, (f"out2_{l}", s, t))

        def pe_extras(pe, l):
            pe.wait_ge(named("x_normed"), 2 * l + 1)
            pe_turn(pe, ("turn", 2 * l + 1), x_tm)
            h_written(pe, ("turn", 2 * l + 1))
            pe.wait_ge(named("ple_loaded"), 16 * (l + 1))
            ps = fill(pe, ("pleT", l), next_bank())
            for k in range(2):
                for t in range(T):
                    ins = pe.transpose(ps[:, k * S + t * P:k * S + (t + 1) * P], PLE_TM[:, t, k * P:(k + 1) * P], ident)
            filled(ins, ("pleT", l))
            for s in range(2):
                w = slab(pe, (f"plegate_{l}", s))
                for t in range(T):
                    product_tm(pe, ("pg", l, s, t), next_bank(), w, 512, 0, 512, h_cm, KD, t)
                released((f"plegate_{l}", s), ("pg", l, s, 1))
            drained(pe, ("pleT", l))
            w = slab(pe, (f"pleproj_{l}", 0))
            for s in range(2):
                for t in range(T):
                    product_tm(pe, ("pp", l, s, t), next_bank(), w, 1024, 512 * s, 512, PLE_CM, 2, t)
            released((f"pleproj_{l}", 0), ("pp", l, 1, 1))
            if l == 1:
                pe.wait_ge(named("router_loaded"), 16)
                ps = fill(pe, ("rt",), next_bank())
                for t in range(T):
                    for k in range(KD):
                        ins = pe.matmul(ps[:, t * 8:(t + 1) * 8], h_cm[:, k, t * P:(t + 1) * P], ROUTER[:, k * 8:(k + 1) * 8],
                                        start=k == 0, stop=k == KD - 1)
                filled(ins, ("rt",))
                pe.wait_ge(named("routed"), 1)
                ps = fill(pe, ("rank",), next_bank())
                for c0, lhs, t, start, stop_ in ((0, "tokens_upto", 0, True, True), (8, "ones", 0, True, False),
                                                 (8, "tokens_upto", 1, False, True), (16, "ones", 0, True, False),
                                                 (16, "ones", 1, False, True)):
                    ins = pe.matmul(ps[:, c0:c0 + 8], const(lhs, P), RT[4][:, t, :], start=start, stop=stop_)
                filled(ins, ("rank",))

        def act_extras(act, ch, l):
            act_turned(act, ("turn", 2 * l + 1), None)
            for s in range(2):
                for t in range(T):
                    ps = full(act, ("pg", l, s, t))
                    free(act.activation(E_TM[:, t, s * 512:(s + 1) * 512], ps[:, :], ACT.Sigmoid), ("pg", l, s, t))
            if l == 1:
                act.wait_ge(named("top_two"), 1)
                act.activation(RC[4], RC[3], ACT.Exp).then_inc(named("top_exp"), 1)

        def dve_extras(dve, ch, l):
            v = nc.vector
            dve_turned(dve, ("turn", 2 * l + 1), None)
            ps = full(dve, ("pleT", l))
            free(v.tensor_copy(PLE_CM, ps[:, :].rearrange("p (k s) -> p k s", s=S)), ("pleT", l))
            for s in range(2):
                for t in range(T):
                    drained(dve, ("pg", l, s, t))
                    ps = full(dve, ("pp", l, s, t))
                    part = E_TM[:, t, s * 512:(s + 1) * 512]
                    free(v.tensor_tensor(part, part, ps[:, :], ALU.mult), ("pp", l, s, t))
                    drained(dve, ("pp", l, s, t))
            ch.step(v.scalar_tensor_tensor(E_TM, x_tm[:, :, :], ALPHA, E_TM, ALU.mult, ALU.add))
            if l == 1:
                dve_router(dve, ch)

        def dve_router(dve, ch):
            v = nc.vector
            ps = full(dve, ("rt",))
            free(v.tensor_copy(LOGITS, ps[:, 0:16].rearrange("p (t e) -> p t e", t=T)), ("rt",))
            drained(dve, ("rt",))
            src = LOGITS
            order = times(const("order", 8), T)
            for r in range(2):
                top, first, hot, place = RC[r], RC[5], RT[r], RT[2]
                ch.step(v.tensor_reduce(top, src, AX, ALU.max))
                ch.step(v.tensor_tensor(place, src, spread(top, 8), ALU.is_equal))
                ch.step(v.tensor_tensor(place, place, order, ALU.mult))
                ch.step(v.tensor_reduce(first, place, AX, ALU.max))
                ch.step(v.tensor_tensor(hot, place, spread(first, 8), ALU.is_equal))
                if r == 0:
                    ch.step(v.scalar_tensor_tensor(RT[3], hot, -3e38, LOGITS, ALU.mult, ALU.add))
                    src = RT[3]
            v.tensor_tensor(RC[3], RC[1], RC[0], ALU.subtract).then_inc(named("top_two"), 1)
            dve.wait_ge(named("top_exp"), 1)
            v.tensor_tensor(RT[4], RT[0], RT[1], ALU.add).then_inc(named("routed"), 1)
            dve.wait_ge(named("routed"), 1)
            ch.step(v.tensor_scalar(RC[5], RC[4], 1.0, None, ALU.add))
            ch.step(v.reciprocal(RC[6], RC[5]))
            ch.step(v.tensor_tensor(RC[7], RC[4], RC[6], ALU.mult))
            ch.step(v.tensor_tensor(RT[0], RT[0], spread(RC[6], 8), ALU.mult))
            ch.step(v.tensor_tensor(RT[1], RT[1], spread(RC[7], 8), ALU.mult))
            ch.step(v.tensor_tensor(COMB, RT[0], RT[1], ALU.add))
            ps = full(dve, ("rank",))
            ch.add(v.tensor_tensor(PLACE, ps[:, 0:16].rearrange("p (t e) -> p t e", t=T), RT[4], ALU.mult))
            free(v.tensor_copy(QUEUED, ps[:, 16:24]), ("rank",))
            drained(dve, ("rank",))
            ch.add(v.tensor_reduce(LONGEST, QUEUED, AX, ALU.max))
            ch.fence()
            for i in range(MAX_PASSES - 1):
                ch.add(v.tensor_scalar(OVER[:, i:i + 1], LONGEST, float(PLACES * (i + 1)), None, ALU.is_gt))
            ch.fence()
            ch.step(v.tensor_reduce(LONGEST, OVER, AX, ALU.add))
            v.tensor_scalar(PASSES, LONGEST, 1.0, None, ALU.add).then_inc(named("passes_known"), 1)
            ch.step(v.tensor_scalar(PLACE, PLACE, -1.0, None, ALU.add))

        def dve_dense_end(dve):
            full_sum(dve, "dense")
            for i in range(4):
                t, half = divmod(i, 2)
                c = slice(half * 512, half * 512 + 512)
                free(nc.vector.tensor_tensor(x_tm[:, t, c], E_TM[:, t, c], PS[4 + i][:, :], ALU.add), ("dense", i))
            x_after("dense")(dve)

        GATHERS = 2 * KD
        TURNED = 4
        ALL_UNITS = N_EXPERTS * U_EXPERT
        LOAD_ROUNDS = 2 * ALL_UNITS // SLOTS

        def passes(eng):
            eng.wait_ge(named("passes_known"), 1)
            return eng.value_load(PASSES[0:1, 0:1], min_val=1, max_val=MAX_PASSES)

        def pe_moe_unit_up(pe, par, e, n, loads, s):
            pe.wait_ge(slot_loaded[s], 16 * loads)
            pe.wait_ge(silu_ready, n - 1)
            for half, bank, ready in ((0, PS[par], gate_ready), (1, PS[2 + par], up_ready)):
                if half:
                    pe.wait_ge(hidden_ready, n - 1)
                for m in range(2):
                    for k in range(KD):
                        c0 = k * 512 + half * UNIT + m * P
                        ins = pe.matmul(bank[:, m * PLACES:(m + 1) * PLACES], slot[s][:, c0:c0 + P],
                                        QUEUE[:, bass.ds(e, 1), k, :], start=k == 0, stop=k == KD - 1)
                ins.then_inc(ready, 1)

        def pe_moe_unit_down(pe, par, n, loads, s, start=False, stop=False):
            pe.wait_ge(slot_loaded[s], 16 * loads)
            pe.wait_ge(hidden_ready, n + 1)
            for half in range(2):
                for kk in range(2):
                    ins = pe.matmul(PS[4 + half][0:PLACES, :], ff[:, 2 + par, kk * PLACES:(kk + 1) * PLACES],
                                    slot[s][:, kk * D + half * 512:kk * D + half * 512 + 512],
                                    start=start and kk == 0, stop=stop and kk == 1, skip_group_check=True)
            ins.then_inc(down_done, 1)

        def pe_experts(pe):
            L, n0 = first_load["experts"], unit_base["experts"]
            gathered, scattered = named("moe_bank_filled"), named("moe_scattered")
            for b in range(8):
                pe.wait_ge(psum_free[b], turns[b])
            assert 2 * U_EXPERT % SLOTS == 0
            with pe.Fori(0, passes(pe)) as p:
                pe.wait_ge(named("pick_ready"), p + 1)
                for j in range(GATHERS + TURNED):
                    ps = PS[j % 8]
                    if j >= 8:
                        pe.wait_ge(named(f"moe_bank_read{j % 2}"), p * ((GATHERS + TURNED) // 2) + (j - 8) // 2 + 1)
                    if j < GATHERS:
                        k, h = divmod(j, 2)
                        for t in range(T):
                            ins = pe.matmul(ps[:, 0:4 * PLACES], x_tm[:, t, k * P:(k + 1) * P], PICK[:, t, 4 * h:4 * h + 4, :],
                                            start=t == 0, stop=t == T - 1)
                    else:
                        if j == GATHERS:
                            pe.wait_ge(named("weight_ready"), p + 1)
                        for i in range(2):
                            for t in range(T):
                                ins = pe.transpose(ps[0:PLACES, i * S + t * P:i * S + (t + 1) * P],
                                                   WEIGHT[:, t, 2 * (j - GATHERS) + i, :], ident)
                    ins.then_inc(gathered, 1)
                with pe.Fori(0, N_EXPERTS) as e:
                    first = p * ALL_UNITS + e * U_EXPERT + n0
                    first_round = p * LOAD_ROUNDS + e * (2 * U_EXPERT // SLOTS)

                    def up(i, j):
                        at = L + 2 * j
                        pe_moe_unit_up(pe, (n0 + j) % 2, e, first + j + 2 * i, first_round + (at // SLOTS + 1) + i,
                                       at % SLOTS)

                    def down(i, j, **kw):
                        at = L + 2 * j + 1
                        pe_moe_unit_down(pe, (n0 + j) % 2, first + j + 2 * i, first_round + (at // SLOTS + 1) + i,
                                         at % SLOTS, **kw)

                    for b in range(2):
                        pe.wait_ge(named(f"moe_bank_read{b}"), p * ((GATHERS + TURNED) // 2) + (GATHERS + TURNED) // 2)
                    up(0, 0)
                    up(0, 1)
                    for half in range(2):
                        pe.wait_ge(psum_free[4 + half], p * N_EXPERTS + e + turns[4 + half])
                    down(0, 0, start=True)
                    with pe.Fori(0, U_EXPERT // 2 - 1) as i:
                        up(i, 2)
                        down(i, 1)
                        up(i, 3)
                        down(i, 2)
                    down(U_EXPERT // 2 - 1, 1, stop=True)
                pe.wait_ge(hidden_ready, p * ALL_UNITS + n0 + ALL_UNITS)
                for half in range(2):
                    pe.wait_ge(psum_free[4 + half], p * N_EXPERTS + N_EXPERTS + turns[4 + half])
                for b in range(4):
                    t, half = divmod(b, 2)
                    for e in range(N_EXPERTS):
                        ins = pe.matmul(PS[b][:, :], RETURN[:, e, t * P:(t + 1) * P],
                                        SUMS[:, e, half * 512:half * 512 + 512], start=e == 0, stop=e == N_EXPERTS - 1)
                    ins.then_inc(scattered, 1)

        def moe_bank(eng, j, p, copy):
            eng.wait_ge(named("moe_bank_filled"), p * (GATHERS + TURNED) + j + 1)
            if j < GATHERS:
                k, h = divmod(j, 2)
                ins = copy(QUEUE[:, 4 * h:4 * h + 4, k, :], PS[j % 8][:, 0:4 * PLACES].rearrange("p (e s) -> p e s", s=PLACES))
            else:
                i = 2 * (j - GATHERS)
                ins = copy(RETURN[:, i:i + 2, :], PS[j % 8][0:PLACES, :].rearrange("p (e s) -> p e s", s=S))
            ins.then_inc(named(f"moe_bank_read{j % 2}"), 1)

        def act_experts(act):
            n0 = unit_base["experts"]
            with act.Fori(0, passes(act)) as p:
                for j in range(0, GATHERS + TURNED, 2):
                    moe_bank(act, j, p, act.copy)
                with act.Fori(0, N_EXPERTS) as e:
                    with act.Fori(0, U_EXPERT // 2) as i:
                        for j in range(2):
                            n = p * ALL_UNITS + e * U_EXPERT + n0 + j + 2 * i
                            par = (n0 + j) % 2
                            act.wait_ge(gate_ready, n + 1)
                            act.wait_ge(hidden_ready, n - 1)
                            act.activation(ff[:, par, 0:2 * PLACES], PS[par][:, 0:2 * PLACES], ACT.Silu).then_inc(silu_ready, 1)
                    act.wait_ge(down_done, p * ALL_UNITS + e * U_EXPERT + n0 + U_EXPERT)
                    act.copy(SUMS[:, bass.ds(e, 1), 0:512], PS[4][0:PLACES, :].unsqueeze(1)).then_inc(psum_free[4], 1)

        def dve_experts(dve, ch):
            n0 = unit_base["experts"]
            v = nc.vector
            with dve.Fori(0, passes(dve)) as p:
                places = const("places", PLACES).unsqueeze(1).unsqueeze(1).broadcast_to([P, T, N_EXPERTS, PLACES])
                v.tensor_tensor(PICK, places, spread(PLACE, PLACES), ALU.is_equal).then_inc(named("pick_ready"), 1)
                dve.wait_ge(named("pick_ready"), p + 1)
                v.tensor_tensor(WEIGHT, PICK, spread(COMB, PLACES), ALU.mult).then_inc(named("weight_ready"), 1)
                v.tensor_scalar(PLACE, PLACE, -float(PLACES), None, ALU.add).then_inc(named("places_moved"), 1)
                for j in range(1, GATHERS + TURNED, 2):
                    moe_bank(dve, j, p, v.tensor_copy)
                with dve.Fori(0, N_EXPERTS) as e:
                    with dve.Fori(0, U_EXPERT // 2) as i:
                        for j in range(2):
                            n = p * ALL_UNITS + e * U_EXPERT + n0 + j + 2 * i
                            par = (n0 + j) % 2
                            dve.wait_ge(up_ready, n + 1)
                            dve.wait_ge(silu_ready, n + 1)
                            dve.wait_ge(down_done, n - 1)
                            v.tensor_tensor(ff[:, 2 + par, 0:2 * PLACES], ff[:, par, 0:2 * PLACES],
                                            PS[2 + par][:, 0:2 * PLACES], ALU.mult
                                            ).then_inc(hidden_ready, 1)
                    dve.wait_ge(down_done, p * ALL_UNITS + e * U_EXPERT + n0 + U_EXPERT)
                    v.tensor_copy(SUMS[:, bass.ds(e, 1), 512:1024], PS[5][0:PLACES, :].unsqueeze(1)
                                  ).then_inc(psum_free[5], 1)
                for b in range(4):
                    t, half = divmod(b, 2)
                    part = E_TM[:, t, half * 512:half * 512 + 512]
                    dve.wait_ge(named("moe_scattered"), p * 4 + b + 1)
                    v.tensor_tensor(part, part, PS[b][:, :], ALU.add).then_inc(named("moe_added"), 1)
                dve.wait_ge(named("moe_added"), p * 4 + 4)
                dve.wait_ge(named("places_moved"), p + 1)
            ch.step(v.tensor_copy(x_tm[:, :, :], E_TM))

        def sp_experts(sp):
            L, n0 = first_load["experts"], unit_base["experts"]
            source = dram["experts"]

            def load(part, j, i=0, p=0, peeled=False):
                c0, c1, used = ((0, 4096, up_ready), (4096, 6144, down_done))[part]
                at = L + 2 * j + part
                if peeled:
                    sp.wait_ge(*last_reader[at - SLOTS])
                else:
                    sp.wait_ge(used, p * ALL_UNITS + 2 * i + j + n0 - 1)
                sp.dma_start(slot[at % SLOTS][:, 0:c1 - c0], source[i * 2 + j][:, c0:c1]
                             ).then_inc(slot_loaded[at % SLOTS], 16)

            def two_units(i, p):
                load(0, 1, i, p)
                load(1, 0, i, p)
                load(0, 2, i, p)
                load(1, 1, i, p)

            def last_unit(p):
                load(0, 1, ALL_UNITS // 2 - 1, p)
                load(1, 0, ALL_UNITS // 2 - 1, p)
                load(1, 1, ALL_UNITS // 2 - 1, p)

            load(0, 0, peeled=True)
            load(0, 1, peeled=True)
            load(1, 0, peeled=True)
            load(0, 2)
            load(1, 1, peeled=True)
            with sp.Fori(1, ALL_UNITS // 2 - 1) as i:
                two_units(i, 0)
            last_unit(0)
            needed = passes(sp)
            with sp.If(needed > 1):
                with sp.Fori(1, needed) as p:
                    load(0, 0, 0, p)
                    with sp.Fori(0, ALL_UNITS // 2 - 1) as i:
                        two_units(i, p)
                    last_unit(p)

        block = ctx.enter_context(nc.Block())

        @block.tensor
        def _(pe):
            pe.wait_ge(named("consts_loaded"), 64)
            pe_norm(pe, "ffn1")
            h_written(pe, ("norm", "ffn1"))
            pe_ffn(pe, "ffn1")
            pe_norm(pe, "mix")
            pe_rwkv_in(pe)
            pe_rwkv_chunks(pe)
            pe_attn(pe)
            pe_merge1(pe)
            pe_norm(pe, "ffn2")
            h_written(pe, ("norm", "ffn2"))
            pe_ffn(pe, "ffn2")
            pe_mixer2(pe, 0)
            pe_extras(pe, 0)
            pe_ffn(pe, "dense")
            pe_mixer2(pe, 1)
            pe_extras(pe, 1)
            pe_experts(pe)

        @block.scalar
        def _(act):
            ch = Chain(act, named("act_chain"))
            act.wait_ge(named("consts_loaded"), 64)
            act_norm(act, ch, "ffn1", lambda eng: eng.wait_ge(named("x_loaded"), 16))
            act_ffn(act, "ffn1")
            act_norm(act, ch, "mix", x_after("ffn1"))
            act_rwkv_in(act, ch)
            act_rwkv_chunks(act, ch)
            act_attn(act, ch)
            act_norm(act, ch, "ffn2", x_after_out)
            act_tables(act, ch)
            act_ffn(act, "ffn2")
            for l in range(DEPTH_2):
                act_mixer2(act, ch, l)
                act_layernorm(act, 2 * l)
                act_extras(act, ch, l)
                if l == 0:
                    act_ffn(act, "dense")
                else:
                    act_experts(act)
                act_layernorm(act, 2 * l + 1)

        @block.vector
        def _(dve):
            ch = Chain(dve, named("dve_chain"))
            dve.wait_ge(named("consts_loaded"), 64)
            dve.wait_ge(named("x_loaded"), 16)
            dve_norm(dve, ch, "ffn1")
            dve_ffn(dve, "ffn1")
            dve_add_half(dve, "ffn1")
            dve_norm(dve, ch, "mix")
            dve_rwkv_in(dve, ch)
            dve_rwkv_chunks(dve, ch)
            dve_attn(dve, ch)
            dve_merge1(dve, ch)
            dve_norm(dve, ch, "ffn2")
            dve_tables(dve, ch)
            dve_ffn(dve, "ffn2", dve_bias)
            dve_add_half(dve, "ffn2")
            for l in range(DEPTH_2):
                dve_mixer2(dve, ch, l)
                dve_layernorm(dve, ch, 2 * l)
                dve_extras(dve, ch, l)
                if l == 0:
                    dve_ffn(dve, "dense")
                    dve_dense_end(dve)
                else:
                    dve_experts(dve, ch)
                dve_layernorm(dve, ch, 2 * l + 1)

        @block.gpsimd
        def _(pool):
            ch = Chain(pool, named("pool_chain"))
            pool.wait_ge(named("y_a_ready"), 1)
            pool.dma_start(turn_consts[:, 0:3 * KEYS], dram["c_dilated"]).then_inc(named("masks_loaded"), 16)
            x_after_out(pool)
            pool.dma_start(turn_consts[:, 0:CONSTANTS["causal"].shape[1]], dram["c_causal"]).then_inc(named("tables_loaded"), 16)
            pool.dma_start(POSI[:, 0:256], dram["positions"].broadcast_to([P, S])).then_inc(named("tables_loaded"), 16)
            pool.dma_start(POSI[:, 256:258], dram["positions_q"]).then_inc(named("tables_loaded"), 16)
            pool.dma_start(TAB, dram["rel_table"].broadcast_to([P, 256])).then_inc(named("tables_loaded"), 16)
            pool.dma_start(arena[:, 2560:3072], dram["lambdas"].broadcast_to([P, 512])).then_inc(named("tables_loaded"), 16)
            pool_layernorm(pool, 0)
            for l in range(DEPTH_2):
                pool_extras(pool, l)
                pool_layernorm(pool, 2 * l + 1)
                if l == 0:
                    pool_layernorm(pool, 2)

        @block.sync
        def _(sp):
            sp.dma_start(consts[:, :], dram["c_always"]).then_inc(named("consts_loaded"), 16)
            sp.dma_start(turn_consts[:, :], dram["c_rwkv"]).then_inc(named("consts_loaded"), 16)
            sp.dma_start(CARRY, dram["c_carry"]).then_inc(named("consts_loaded"), 16)
            sp.dma_start(cols[:, :], dram["columns"]).then_inc(named("consts_loaded"), 16)
            sp.dma_start(x_tm[:, :, :], dram["x"]).then_inc(named("x_loaded"), 16)
            sp.dma_start(arena[:, 20480:21504], dram["lora_wa"]).then_inc(named("lora_loaded"), 16)
            sp.dma_start(arena[:, 18432:19456], dram["lora_g"]).then_inc(named("lora_loaded"), 16)
            sp.dma_start(arena[0:32, 19456:20480], dram["lora_g2"]).then_inc(named("lora_loaded"), 16)
            for key, *rest in stream:
                if key in ("ffn", "experts"):
                    if key == "ffn":
                        sp_ffn(sp, rest[0], dram[rest[0]])
                    else:
                        sp_experts(sp)
                    continue
                load = first_load[key]
                source, width = rest
                if load >= SLOTS:
                    sp.wait_ge(*last_reader[load - SLOTS])
                sp.dma_start(slot[load % SLOTS][:, 0:width], source).then_inc(slot_loaded[load % SLOTS], 16)
            sp.wait_ge(named("x_normed"), 2 * DEPTH_2)
            sp.dma_start(out, x_tm[:, :, :]).then_inc(named("out_stored"), 16)
            sp.wait_ge(named("out_stored"), 16)


def laid_out(inputs):
    w = {k: np.asarray(v) for k, v in inputs.items()}

    def rows(a, k):
        n = a.shape[1]
        return a.reshape(k, P, n).transpose(1, 0, 2).reshape(P, k * n)

    def slabs(a, width):
        k = a.shape[0] // P
        return np.ascontiguousarray(a.reshape(k, P, -1, width).transpose(2, 1, 0, 3).reshape(-1, P, k * width))

    def units(gate, up, down):
        n = gate.shape[1] // UNIT
        a = np.stack([gate.reshape(KD, P, n, UNIT), up.reshape(KD, P, n, UNIT)], 3)
        a = a.transpose(2, 1, 0, 3, 4).reshape(n, P, KD * 2 * UNIT)
        b = down.reshape(n, 2, P, D).transpose(0, 2, 1, 3).reshape(n, P, 2 * D)
        return np.concatenate([a, b], 2)

    arrays = {}
    for f in ("ffn1", "ffn2"):
        w_in = w[f"{f}_w_in"][0]
        arrays[f] = units(w_in[:, :F_DENSE], w_in[:, F_DENSE:], w[f"{f}_w_out"][0])
    arrays["dense"] = units(w["dense_w1_2"][0], w["dense_w3_2"][0], w["dense_w2_2"][0])
    arrays["experts"] = np.concatenate([units(w["expert_w1_2"][0, e], w["expert_w3_2"][0, e], w["expert_w2_2"][0, e])
                                        for e in range(N_EXPERTS)])
    w_in = w["w_in"][0]
    at = np.cumsum([0, 3 * D, 288, 768, 768, 768, 2 * D])
    rkv, lora, q, k, v, g = (w_in[:, a:b] for a, b in zip(at[:-1], at[1:]))
    arrays["w_in_a"] = slabs(lora, 288)
    arrays["w_in_rkv"] = slabs(rkv, 512)
    arrays["w_in_gates"] = slabs(g, 512)
    arrays["w_in_v0"] = slabs(v[:, 0:512], 512)
    arrays["w_in_v1"] = slabs(v[:, 512:768], 256)
    arrays["w_in_qk"] = slabs(np.concatenate([q, k], 1), 512)
    arrays["w_proj_rwkv"] = slabs(w["w_proj_rwkv"][0], 512)
    arrays["w_proj_attn"] = slabs(w["w_proj_attn"][0], 512)
    arrays["w_out"] = slabs(w["w_out"][0], 512)
    half = np.arange(32).reshape(2, 16)[::-1].reshape(-1)
    for l in range(DEPTH_2):
        z = w["w_in_2"][l]
        at = np.cumsum([0, 1024, 1024, 1024, 384, 256, 32, 2048])
        dq, dk, dv, cq, ckv, kr, g = (z[:, a:b] for a, b in zip(at[:-1], at[1:]))
        arrays[f"lat_{l}"] = slabs(np.concatenate([cq, ckv[:, 0:128]], 1), 512)
        arrays[f"latr_{l}"] = slabs(np.concatenate([ckv[:, 128:256], kr, kr[:, half]], 1), 192)
        arrays[f"dv_{l}"] = slabs(dv, 512)
        arrays[f"dqk_{l}"] = slabs(np.concatenate([dq, dk], 1), 512)
        arrays[f"g2_{l}"] = slabs(g, 512)
        uq = w["w_uq_2"][l]
        heads = uq.reshape(384, MHEADS, 96)
        arrays[f"uq_{l}"] = slabs(np.concatenate([uq, heads[:, :, 64:][:, :, half].reshape(384, 256)], 1), 1024)
        ukv = w["w_ukv_2"][l].reshape(256, MHEADS, 2, 64)
        arrays[f"ukv_{l}"] = slabs(ukv.transpose(0, 2, 1, 3).reshape(256, 1024), 1024)
        arrays[f"bdiff_{l}"] = slabs(w["w_branch_diff_2"][l], 512)
        arrays[f"bmla_{l}"] = slabs(w["w_branch_mla_2"][l], 1024)
        arrays[f"out2_{l}"] = slabs(w["w_out_2"][l], 512)
        arrays[f"plegate_{l}"] = slabs(w["w_ple_gate_2"][l], 512)
        arrays[f"pleproj_{l}"] = slabs(w["w_ple_proj_2"][l], 1024)
    arrays["lora_wa"] = np.concatenate([w["rwkv_w2"][0], w["rwkv_a2"][0]])
    arrays["lora_g"] = w["rwkv_g2"][0, 0:128]
    arrays["lora_g2"] = w["rwkv_g2"][0, 128:160]
    arrays["router"] = rows(w["router_w_2"][0], KD)
    arrays["ple"] = w["p_2"][:, 0].reshape(DEPTH_2, T, P, 256).transpose(0, 2, 1, 3)
    arrays["x"] = w["x"][0].reshape(T, P, D).transpose(1, 0, 2)
    for which, a in CONSTANTS.items():
        arrays[f"c_{which}"] = a
    arrays["rel_table"] = w["rel_bias_table_2"].reshape(1, 256)
    arrays["positions"] = w["positions_2"].reshape(1, S)
    arrays["positions_q"] = w["positions_2"].reshape(T, P).T
    arrays["lambdas"] = np.stack([w[f"lambda_{n}_2"] for n in ("q1", "k1", "q2", "k2")], 1).reshape(1, 512)
    arrays["ln_gain"] = np.stack([w["ln_mix_g_2"], w["ln_ffn_g_2"]], 1).reshape(2 * DEPTH_2, D)
    arrays["ln_bias"] = np.stack([w["ln_mix_b_2"], w["ln_ffn_b_2"]], 1).reshape(2 * DEPTH_2, D)

    mu = w["rwkv_mu"][0]
    twice = lambda a: np.concatenate([a, a])
    vectors = [w["ffn1_norm"][0], w["mix_norm"][0], w["ffn2_norm"][0], w["b_gate"][0], mu[0:3072], mu[3072:3200],
               mu[3200:3328], np.tile(mu[3328:3360], 4), w["rwkv_w0"][0], w["rwkv_a0"][0], w["rwkv_k_k"][0],
               w["rwkv_k_a"][0], w["rwkv_r_k"][0].reshape(-1), w["rwkv_ln_w"][0], w["rwkv_ln_b"][0],
               twice(w["attn_q_norm"][0]), twice(w["attn_k_norm"][0])]
    for l in range(DEPTH_2):
        vectors += [w["b_gate_2"][l], w["diff_subln_g_2"][l], w["mla_q_norm_g_2"][l], w["mla_kv_norm_g_2"][l]]
    arrays["columns"] = np.concatenate(vectors).reshape(N_COLS, P).T

    return {n: np.ascontiguousarray(a) for n, a in arrays.items()}


def kernel(**inputs):
    import concourse.bacc as bacc
    from concourse.bass_utils import run_bass_kernel_spmd

    nc = bacc.Bacc("TRN2", target_bir_lowering=False, num_devices=1)
    arrays = laid_out(inputs)
    dram = {n: nc.dram_tensor(f"in_{n}", a.shape, mybir.dt.from_np(a.dtype), kind="ExternalInput").ap()
            for n, a in arrays.items()}
    out = nc.dram_tensor("out", (P, T, D), F32, kind="ExternalOutput").ap()
    two_blocks(nc, dram, out)
    r = run_bass_kernel_spmd(nc, [{f"in_{n}": a for n, a in arrays.items()}], core_ids=[0])
    return r.results[0]["out"].transpose(1, 0, 2).reshape(1, S, D)
```
